# Optimizing a Trainium2 kernel written in Bass

```python
import math
import jax, jax.numpy as jnp
from jax import lax
import numpy as np

D_MODEL = 1024
BATCH = 1
SEQ = 1024
DEPTH = 1
DEC_BATCH = 8
DEC_SEQ = 1
PAST_LEN = 4096
PAGE_SIZE = 128

H_A = 4
DK_A = 32
DV_A = 2 * DK_A
W_A = H_A * DV_A
Q_BLOCK = 128
D_LRU = D_MODEL // 2
N_LRU_BLOCKS = 8
LRU_BLOCK = D_LRU // N_LRU_BLOCKS
CONV_W = 4
LRU_C = 8.0
H_C = 4
DH_C = 64
W_C = H_C * DH_C
DIL_PATTERNS = ((128, 1), (512, 4), (2048, 16))
MAX_WINDOW = 2048
D_MIX = W_A + D_LRU + W_C
SPLIT_SIZES = (W_A, W_A, W_A, W_A, D_LRU, D_LRU, W_C, W_C, W_C, W_C)
D_IN = sum(SPLIT_SIZES)
RMS_EPS = 1e-6

kernel_name = "hymba_diffattn_rglru_dilated_step"

def rms_norm(x, g):
    xf = x.astype(jnp.float32)
    y = xf * lax.rsqrt(jnp.mean(xf * xf, axis=-1, keepdims=True) + RMS_EPS)
    return (y * g.astype(jnp.float32)).astype(x.dtype)

def project(x, ln_pre, w_in):
    u = rms_norm(x, ln_pre) @ w_in
    offsets = [int(o) for o in np.cumsum(SPLIT_SIZES)[:-1]]
    return jnp.split(u, offsets, axis=-1)

def heads(x, d):
    return x.reshape(*x.shape[:-1], -1, d)

def heads_qk(x):
    return x.reshape(*x.shape[:-1], H_A, 2, DK_A)

def diff_lambda(lq1, lk1, lq2, lk2, lam_init):
    f = jnp.float32
    return (jnp.exp(jnp.sum(lq1.astype(f) * lk1.astype(f)))
            - jnp.exp(jnp.sum(lq2.astype(f) * lk2.astype(f))) + lam_init)

def diff_attn_prompt(q, k, v, lam):
    b, s = q.shape[:2]
    nblk = s // Q_BLOCK
    scale = DK_A ** -0.5
    qb = jnp.moveaxis(q.reshape(b, nblk, Q_BLOCK, H_A, 2, DK_A), 1, 0)
    kpos = jnp.arange(s)

    def one_block(args):
        qblk, q0 = args
        sc = jnp.einsum("bqhcd,bkhcd->bhcqk", qblk, k).astype(jnp.float32) * scale
        qpos = q0 + jnp.arange(Q_BLOCK)
        sc = jnp.where(kpos[None, :] <= qpos[:, None], sc, -jnp.inf)
        p = jax.nn.softmax(sc, axis=-1)
        pd = p[:, :, 0] - lam * p[:, :, 1]
        return jnp.einsum("bhqk,bkhd->bqhd", pd.astype(v.dtype), v)

    out = lax.map(one_block, (qb, jnp.arange(nblk) * Q_BLOCK))
    return jnp.moveaxis(out, 0, 1).reshape(b, s, H_A, DV_A)

def diff_attn_sample(q, k_new, v_new, k_past, v_past, lam):
    t = q.shape[1]
    p_len = k_past.shape[1]
    scale = DK_A ** -0.5
    s_past = jnp.einsum("bqhcd,bkhcd->bhcqk", q, k_past).astype(jnp.float32) * scale
    s_new = jnp.einsum("bqhcd,bkhcd->bhcqk", q, k_new).astype(jnp.float32) * scale
    causal = jnp.arange(t)[None, :] <= jnp.arange(t)[:, None]
    s_new = jnp.where(causal, s_new, -jnp.inf)
    p = jax.nn.softmax(jnp.concatenate([s_past, s_new], axis=-1), axis=-1)
    pd = (p[:, :, 0] - lam * p[:, :, 1]).astype(v_new.dtype)
    return (jnp.einsum("bhqk,bkhd->bqhd", pd[..., :p_len], v_past)
            + jnp.einsum("bhqk,bkhd->bqhd", pd[..., p_len:], v_new))

def causal_conv(x, buf, w, b):
    t = x.shape[1]
    xp = jnp.concatenate([buf, x], axis=1)
    y = xp[:, 0:t] * w[0]
    for i in range(1, CONV_W):
        y = y + xp[:, i:i + t] * w[i]
    return y + b, xp[:, -(CONV_W - 1):]

def block_diag_linear(x, w, b):
    xb = x.reshape(*x.shape[:-1], N_LRU_BLOCKS, LRU_BLOCK)
    y = jnp.einsum("...nd,nde->...ne", xb, w)
    return y.reshape(x.shape) + b

def rg_lru(x, h0, w_r, b_r, w_i, b_i, lru_lambda):
    f = jnp.float32
    r_gate = jax.nn.sigmoid(block_diag_linear(x, w_r, b_r).astype(f))
    i_gate = jax.nn.sigmoid(block_diag_linear(x, w_i, b_i).astype(f))
    log_a = -LRU_C * r_gate * jax.nn.softplus(-lru_lambda.astype(f))
    a = jnp.exp(log_a)
    bterm = jnp.sqrt(-jnp.expm1(2.0 * log_a)) * (i_gate * x.astype(f))
    bterm = bterm.at[:, 0].add(a[:, 0] * h0.astype(f))

    def combine(left, right):
        a1, b1 = left
        a2, b2 = right
        return a1 * a2, a2 * b1 + b2

    _, h = lax.associative_scan(combine, (a, bterm), axis=1)
    return h.astype(x.dtype), h[:, -1].astype(x.dtype)

def band_attn(q, k, v, blk):
    n, l = q.shape[:2]
    nb = l // blk
    scale = DH_C ** -0.5
    qb = q.reshape(n, nb, blk, H_C, DH_C)
    kb = k.reshape(n, nb, blk, H_C, DH_C)
    vb = v.reshape(n, nb, blk, H_C, DH_C)
    k2 = jnp.concatenate([jnp.concatenate([jnp.zeros_like(kb[:, :1]), kb[:, :-1]], axis=1), kb], axis=2)
    v2 = jnp.concatenate([jnp.concatenate([jnp.zeros_like(vb[:, :1]), vb[:, :-1]], axis=1), vb], axis=2)
    sc = jnp.einsum("nbqhd,nbkhd->nbhqk", qb, k2).astype(jnp.float32) * scale
    qi = jnp.arange(blk)[:, None] + blk
    kj = jnp.arange(2 * blk)[None, :]
    dist = qi - kj
    band = (dist >= 0) & (dist <= blk)
    started = (jnp.arange(nb)[:, None, None] > 0) | (kj[None] >= blk)
    valid = band[None] & started
    sc = jnp.where(valid[None, :, None], sc, -jnp.inf)
    m = jnp.max(sc, axis=-1, keepdims=True)
    p = jnp.exp(sc - m)
    den = jnp.sum(p, axis=-1)
    num = jnp.einsum("nbhqk,nbkhd->nbqhd", p, v2.astype(jnp.float32))
    num = num.reshape(n, l, H_C, DH_C)
    den = jnp.swapaxes(den, 2, 3).reshape(n, l, H_C)
    m = jnp.swapaxes(m[..., 0], 2, 3).reshape(n, l, H_C)
    return num, den, m

def combine_dilated(parts):
    m_all = jnp.max(jnp.stack([m for _, _, m in parts]), axis=0)
    num = sum(nm * jnp.exp(m - m_all)[..., None] for nm, _, m in parts)
    den = sum(dn * jnp.exp(m - m_all) for _, dn, m in parts)
    return num / den[..., None]

def dilated_prompt(q, k, v):
    b, s = q.shape[:2]
    parts = []
    for window, dil in DIL_PATTERNS:
        blk = window // dil
        s_pad = -(-s // window) * window
        sub_len = s_pad // dil

        def to_sub(x):
            x = jnp.pad(x, ((0, 0), (0, s_pad - s), (0, 0), (0, 0)))
            x = jnp.swapaxes(x.reshape(b, sub_len, dil, H_C, DH_C), 1, 2)
            return x.reshape(b * dil, sub_len, H_C, DH_C)

        def from_sub(y):
            y = jnp.swapaxes(y.reshape(b, dil, sub_len, *y.shape[2:]), 1, 2)
            return y.reshape(b, s_pad, *y.shape[3:])[:, :s]

        num, den, m = band_attn(to_sub(q), to_sub(k), to_sub(v), blk)
        parts.append((from_sub(num), from_sub(den), from_sub(m)))
    return combine_dilated(parts).astype(q.dtype)

def dilated_sample(q, k_new, v_new, k_buf, v_buf):
    wb = k_buf.shape[1]
    t = q.shape[1]
    scale = DH_C ** -0.5
    kk = jnp.concatenate([k_buf, k_new], axis=1)
    vv = jnp.concatenate([v_buf, v_new], axis=1)
    parts = []
    for window, dil in DIL_PATTERNS:
        nk = window // dil + 1
        idx = wb + jnp.arange(t)[:, None] - dil * jnp.arange(nk)[None, :]
        valid = idx >= 0
        idx_c = jnp.maximum(idx, 0)
        kg = kk[:, idx_c]
        vg = vv[:, idx_c]
        sc = jnp.einsum("bthd,btkhd->bthk", q, kg).astype(jnp.float32) * scale
        sc = jnp.where(valid[None, :, None, :], sc, -jnp.inf)
        m = jnp.max(sc, axis=-1)
        p = jnp.exp(sc - m[..., None])
        den = jnp.sum(p, axis=-1)
        num = jnp.einsum("bthk,btkhd->bthd", p, vg.astype(jnp.float32))
        parts.append((num, den, m))
    return combine_dilated(parts).astype(q.dtype)

def merge_branches(x, a_core, b_core, c_core, ga, gb, gc, lam_init, subln_g, w_out, ln_post):
    n, t = x.shape[:2]
    a = (rms_norm(a_core, subln_g) * (1.0 - lam_init)).reshape(n, t, W_A) * jax.nn.silu(ga)
    b = b_core * jax.nn.silu(gb)
    c = c_core.reshape(n, t, W_C) * jax.nn.silu(gc)
    y = jnp.concatenate([a, b, c], axis=-1) @ w_out
    return x + rms_norm(y, ln_post)

def _normal(k, shape, s=1.0):
    return s * jax.random.normal(k, shape, jnp.float32)

def setup_inputs(seed: int = 0) -> dict:
    key = jax.random.key(seed)
    ks = jax.random.split(key, 26)
    n_pages = PAST_LEN // PAGE_SIZE
    n_used = DEC_BATCH * n_pages
    n_pool = n_used + max(1, n_used // 4)
    w_buf = min(MAX_WINDOW, PAST_LEN)
    page_table = jax.random.permutation(ks[0], n_pool)[:n_used].reshape(DEC_BATCH, n_pages).astype(jnp.int32)
    u = jax.random.uniform(ks[1], (DEPTH, D_LRU), jnp.float32, 0.9, 0.999)
    a0 = u ** (1.0 / LRU_C)
    lru_lambda = jnp.log(a0) - jnp.log1p(-a0)
    return {
        "x_prompt": _normal(ks[2], (BATCH, SEQ, D_MODEL)),
        "x_sample": _normal(ks[3], (DEC_BATCH, DEC_SEQ, D_MODEL)),
        "cache_a_k": _normal(ks[4], (DEPTH, n_pool, PAGE_SIZE, H_A, 2 * DK_A)),
        "cache_a_v": _normal(ks[5], (DEPTH, n_pool, PAGE_SIZE, H_A, DV_A)),
        "state_conv": _normal(ks[6], (DEPTH, DEC_BATCH, CONV_W - 1, D_LRU)),
        "state_lru": _normal(ks[7], (DEPTH, DEC_BATCH, D_LRU), 0.5),
        "cache_c_k": _normal(ks[8], (DEPTH, DEC_BATCH, w_buf, H_C, DH_C)),
        "cache_c_v": _normal(ks[9], (DEPTH, DEC_BATCH, w_buf, H_C, DH_C)),
        "page_table": page_table,
        "ln_pre": 1.0 + _normal(ks[10], (DEPTH, D_MODEL), 0.05),
        "ln_post": 1.0 + _normal(ks[11], (DEPTH, D_MODEL), 0.05),
        "w_in": _normal(ks[12], (DEPTH, D_MODEL, D_IN), D_MODEL ** -0.5),
        "w_out": _normal(ks[13], (DEPTH, D_MIX, D_MODEL), D_MIX ** -0.5),
        "lam_q1": _normal(ks[14], (DEPTH, DK_A), 0.1),
        "lam_k1": _normal(ks[15], (DEPTH, DK_A), 0.1),
        "lam_q2": _normal(ks[16], (DEPTH, DK_A), 0.1),
        "lam_k2": _normal(ks[17], (DEPTH, DK_A), 0.1),
        "subln_g": 1.0 + _normal(ks[18], (DEPTH, DV_A), 0.05),
        "conv_w": _normal(ks[19], (DEPTH, CONV_W, D_LRU), CONV_W ** -0.5),
        "conv_b": _normal(ks[20], (DEPTH, D_LRU), 0.01),
        "w_rgate": _normal(ks[21], (DEPTH, N_LRU_BLOCKS, LRU_BLOCK, LRU_BLOCK), LRU_BLOCK ** -0.5),
        "b_rgate": _normal(ks[22], (DEPTH, D_LRU), 0.01),
        "w_igate": _normal(ks[23], (DEPTH, N_LRU_BLOCKS, LRU_BLOCK, LRU_BLOCK), LRU_BLOCK ** -0.5),
        "b_igate": _normal(ks[24], (DEPTH, D_LRU), 0.01),
        "lru_lambda": lru_lambda,
    }

def reference(x_prompt, x_sample, cache_a_k, cache_a_v, state_conv, state_lru, cache_c_k, cache_c_v,
              page_table, ln_pre, ln_post, w_in, w_out, lam_q1, lam_k1, lam_q2, lam_k2, subln_g,
              conv_w, conv_b, w_rgate, b_rgate, w_igate, b_igate, lru_lambda):
    bp, sp = x_prompt.shape[:2]
    bs = x_sample.shape[0]
    n_pages = page_table.shape[1]
    keep_p = min(MAX_WINDOW, sp)
    hp, hs = x_prompt, x_sample
    akp, avp, aks, avs = [], [], [], []
    cnp, cns, lrp, lrs = [], [], [], []
    ckp, cvp, cks, cvs = [], [], [], []
    for l in range(DEPTH):
        lam_init = 0.8 - 0.6 * math.exp(-0.3 * l)
        lam = diff_lambda(lam_q1[l], lam_k1[l], lam_q2[l], lam_k2[l], lam_init)

        qa, ka, va, ga, xb, gb, qc, kc, vc, gc = project(hp, ln_pre[l], w_in[l])
        va4 = heads(va, DV_A)
        a_core = diff_attn_prompt(heads_qk(qa), heads_qk(ka), va4, lam)
        xcv, conv_new = causal_conv(xb, jnp.zeros((bp, CONV_W - 1, D_LRU), xb.dtype), conv_w[l], conv_b[l])
        b_core, h_last = rg_lru(xcv, jnp.zeros((bp, D_LRU), xb.dtype), w_rgate[l], b_rgate[l],
                                w_igate[l], b_igate[l], lru_lambda[l])
        kc4, vc4 = heads(kc, DH_C), heads(vc, DH_C)
        c_core = dilated_prompt(heads(qc, DH_C), kc4, vc4)
        hp = merge_branches(hp, a_core, b_core, c_core, ga, gb, gc, lam_init, subln_g[l], w_out[l], ln_post[l])
        akp.append(heads(ka, 2 * DK_A))
        avp.append(va4)
        cnp.append(conv_new)
        lrp.append(h_last)
        ckp.append(kc4[:, sp - keep_p:])
        cvp.append(vc4[:, sp - keep_p:])

        qa, ka, va, ga, xb, gb, qc, kc, vc, gc = project(hs, ln_pre[l], w_in[l])
        va4 = heads(va, DV_A)
        k_past = cache_a_k[l][page_table].reshape(bs, n_pages * PAGE_SIZE, H_A, 2, DK_A)
        v_past = cache_a_v[l][page_table].reshape(bs, n_pages * PAGE_SIZE, H_A, DV_A)
        a_core = diff_attn_sample(heads_qk(qa), heads_qk(ka), va4, k_past, v_past, lam)
        xcv, conv_new = causal_conv(xb, state_conv[l], conv_w[l], conv_b[l])
        b_core, h_last = rg_lru(xcv, state_lru[l], w_rgate[l], b_rgate[l], w_igate[l], b_igate[l], lru_lambda[l])
        kc4, vc4 = heads(kc, DH_C), heads(vc, DH_C)
        c_core = dilated_sample(heads(qc, DH_C), kc4, vc4, cache_c_k[l], cache_c_v[l])
        hs = merge_branches(hs, a_core, b_core, c_core, ga, gb, gc, lam_init, subln_g[l], w_out[l], ln_post[l])
        aks.append(heads(ka, 2 * DK_A))
        avs.append(va4)
        cns.append(conv_new)
        lrs.append(h_last)
        cks.append(kc4)
        cvs.append(vc4)

    new_a_k_prompt = jnp.stack(akp)
    new_a_v_prompt = jnp.stack(avp)
    new_a_k_sample = jnp.stack(aks)
    new_a_v_sample = jnp.stack(avs)
    new_conv_prompt = jnp.stack(cnp)
    new_conv_sample = jnp.stack(cns)
    new_lru_prompt = jnp.stack(lrp)
    new_lru_sample = jnp.stack(lrs)
    new_c_k_prompt = jnp.stack(ckp)
    new_c_v_prompt = jnp.stack(cvp)
    new_c_k_sample = jnp.stack(cks)
    new_c_v_sample = jnp.stack(cvs)
    return (hp, hs, new_a_k_prompt, new_a_v_prompt, new_a_k_sample, new_a_v_sample,
            new_conv_prompt, new_conv_sample, new_lru_prompt, new_lru_sample,
            new_c_k_prompt, new_c_v_prompt, new_c_k_sample, new_c_v_sample)


_drawn_inputs = setup_inputs


def setup_inputs(seed=0):
    import zlib

    import numpy as np

    out = dict(_drawn_inputs(seed))
    spreads = {}
    factors = {'lam_q1': 3.442,
     'lam_k1': 8.0,
     'lam_q2': 8.0,
     'lam_k2': 5.517,
     'b_rgate': 22.058,
     'b_igate': 8.0}
    for name, (base, spread) in spreads.items():
        noise = np.random.default_rng([zlib.crc32(name.encode()), seed]).standard_normal(out[name].shape)
        drawn = base * np.exp(spread * noise) if base else spread * noise
        out[name] = __import__('jax').numpy.asarray(drawn.astype(out[name].dtype))
    for name, factor in factors.items():
        out[name] = (out[name] * factor).astype(out[name].dtype)
    return out
```

```python
from contextlib import ExitStack

import concourse.bass as bass
from concourse import mybir

P = 128
S = 1024
NB = 8
SW = S + NB
D = 1024
KT = D // P
HA, DKA = 4, 32
HC, DHC = 4, 64
HCA = 2 * HA
W_BR = 256
DL = 512
PAGES, PAGE = 32, 128
QPP = P // PAGES
PPP = PAGE // QPP
CH = 4
NCH = PPP // CH
NK = NB * NCH
SCALE_A, SCALE_C = DKA ** -0.5, DHC ** -0.5
EPS = 1e-6
LAM_INIT = 0.2
NEG = -1.0e30
CW = SW // 3

F32, F32R = mybir.dt.float32, mybir.dt.float32r
I32, U32 = mybir.dt.int32, mybir.dt.uint32
ALU = mybir.AluOpType
ACT = mybir.ActivationFunctionType
AX = mybir.AxisListType.X
RMAX = bass.bass_isa.ReduceOp.max

TILES = [("qa0", 0), ("qa1", 128), ("ka0", 256), ("ka1", 384), ("va0", 512), ("va1", 640),
         ("vc0", 2560), ("vc1", 2688), ("qc0", 2048), ("qc1", 2176), ("kc0", 2304), ("kc1", 2432),
         ("xb0", 1024), ("xb1", 1152), ("xb2", 1280), ("xb3", 1408),
         ("gb0", 1536), ("gb1", 1664), ("gb2", 1792), ("gb3", 1920),
         ("ga0", 768), ("ga1", 896), ("gc0", 2816), ("gc1", 2944)]
NAMES = [n for n, _ in TILES]
NT = len(TILES)
TI = {n: t for t, n in enumerate(NAMES)}
KEPT = ["qa0", "qa1", "qc0", "qc1", "ka0", "ka1", "kc0", "kc1", "xb0", "xb1", "xb2", "xb3"]
PASSING = [n for n in NAMES if n not in KEPT]
GATES = [n for n in NAMES if n[0] == "g"]
GATE_AT = {n: i for i, n in enumerate(GATES)}
MIX = ["qa0", "qa1", "xb0", "xb1", "xb2", "xb3", "qc0", "qc1"]

PSTEPS = NT * KT
K_FIRST, V_LAG = 1, 16


def k_step(n):
    return K_FIRST + (12 * n) // 5


def v_step(m):
    return k_step(m + V_LAG)


K_AT = {k_step(n): n for n in range(NK)}
V_AT = {v_step(m): m for m in range(NK)}
MAX_AT = {max(k_step(NCH * b + NCH - 1), 36 + b): b for b in range(NB)}
assert all(v_step(NCH * b) >= s + 3 for s, b in MAX_AT.items())
PICK_AT = {v_step(NCH * b + NCH - 1) + 4: b for b in range(NB)}
C_STEP = {(13 + b) * KT: b for b in range(NB)}

JOBS = [(8 * 1 + 2, "param", 0, 0), (8 * 1 + 5, "state", 0, 0),
        (8 * 4 + 1, "rows", 0, 0), (8 * 8 + 1, "rows", 1, 0), (8 * 12 + 1, "rows", 2, 0),
        (8 * 16 + 1, "rows", 3, 0), (8 * 16 + 3, "tail", 0, 0)]
for _n in ("ka0", "ka1", "va0", "va1", "vc0", "vc1", "kc0", "kc1"):
    for _h in range(2):
        JOBS.append((8 * (TI[_n] + 1) + 3 + 3 * _h, "turn", _n, _h))
for _s, _b in C_STEP.items():
    JOBS.append((_s + 7, "cpv", _b, 0))
JOBS.sort()
JOB_NO = {(k, a, h): i for i, (_, k, a, h) in enumerate(JOBS)}
JOB_AT = {s: i for i, (s, _, _, _) in enumerate(JOBS)}
TURNS = [j for j in JOBS if j[1] == "turn"]
assert len(JOB_AT) == len(JOBS)

NQ = S // P
UNITS = [(h, q) for h in range(HA + HC) for q in range(NQ)]
NU = len(UNITS)
LRU_AT = {3 + 11 * f: f for f in range(4)}
NORM_AT = {42: 0, 50: 1}

ITEMS = []
for _u in range(-1, NU):
    if _u + 1 < NU:
        ITEMS += [("s", _u + 1, c) for c in range(2 if UNITS[_u + 1][0] < HA else 1)]
    if _u - 1 in LRU_AT:
        ITEMS += [("gate", LRU_AT[_u - 1], w) for w in range(2)]
    if _u - 1 in NORM_AT:
        ITEMS += [("norm", NORM_AT[_u - 1], 0)]
ITEM_NO = {it: i for i, it in enumerate(ITEMS)}
NS_BEFORE = [sum(x[0] == "s" for x in ITEMS[:i + 1]) for i in range(len(ITEMS))]
SCORE_NO = {it: NS_BEFORE[i] - 1 for it, i in ITEM_NO.items() if it[0] == "s"}
OTHER_NO = {it: i - NS_BEFORE[i] for it, i in ITEM_NO.items() if it[0] != "s"}
GROUPS = [(u, g) for u, (h, q) in enumerate(UNITS) for g in range(2 if q >= 4 else 1)]
GROUP_NO = {x: i for i, x in enumerate(GROUPS)}


def build(nc, a, o):
    with ExitStack() as ctx:
        def sem(name):
            return ctx.enter_context(nc.semaphore(name))

        top = [0]

        def at(name, shape, dt=F32):
            size = 4
            for n in shape[1:]:
                size *= n
            size = -(-size // 32) * 32
            t = nc.alloc_sbuf_tensor_at(name, shape, dt, offset=top[0])
            top[0] += size
            return t

        def dram(name, shape):
            return nc.dram_tensor(name, shape, F32, kind="Internal").ap()

        base = -(-nc.sbuf_base // 32) * 32
        top[0] = base
        xh, xl = at("xh", [P, KT, SW], F32R), at("xl", [P, KT, SW], F32R)
        x_end = top[0]
        top[0] = base
        stack = [[at(f"stack{s}{i}", [P, S], F32R) for i in range(4)] for s in range(2)]
        E = [at(f"E{i}", [P, S]) for i in range(4)]
        T = [at(f"T{i}", [P, S]) for i in range(2)]
        PT = [at(f"PT{i}", [P, NQ, P]) for i in range(2)]
        assert top[0] <= x_end
        top[0] = base
        mh, ml = at("mh", [P, KT, SW], F32R), at("ml", [P, KT, SW], F32R)
        w_base = x_end
        top[0] = w_base
        wraw = [at(f"wraw{i}", [P, KT, P]) for i in range(3)]
        wh = [at(f"wh{i}", [P, KT, P], F32R) for i in range(2)]
        wl = [at(f"wl{i}", [P, KT, P], F32R) for i in range(2)]
        passing = [at(f"passing{i}", [P, SW]) for i in range(3)]
        w_end = top[0]
        top[0] = w_base
        mask_a, mask_c = at("mask_a", [P, S]), at("mask_c", [P, S])
        TMP = [at(f"TMP{i}", [P, SW]) for i in range(4)]
        split_base = top[0]
        QH, QL = at("QH", [P, S], F32R), at("QL", [P, S], F32R)
        KH, KL = at("KH", [P, S], F32R), at("KL", [P, S], F32R)
        w_end = max(w_end, top[0])
        top[0] = w_end
        kbuf = [at(f"kbuf{i}", [P, CH, W_BR]) for i in range(2)]
        vbuf = [at(f"vbuf{i}", [P, CH, W_BR]) for i in range(3)]
        prod = at("prod", [P, CH, W_BR])
        sc = [at(f"sc{i}", [P, PPP, HCA]) for i in range(2)]
        ex = [at(f"ex{i}", [P, PPP, HCA]) for i in range(2)]
        qrep = [at(f"qrep{i}", [P, W_BR]) for i in range(2)]
        acc = at("acc", [P, W_BR])
        acc_c = at("acc_c", [P, W_BR])
        qrep_c = at("qrep_c", [P, W_BR])
        prow, srow = at("prow", [NB, DL]), at("srow", [4 * NB, DL])
        top[0] -= 4 * 2 * DL
        kc = at("kc", [P, 3, W_BR])
        vc = [at(f"vc{i}", [P, 3, W_BR]) for i in range(2)]
        s_end = top[0]
        top[0] = s_end - 2 * 4 * KT * D
        assert top[0] >= split_base - 2 * 4 * SW - 64, (top[0], split_base)
        woh, wol = at("woh", [P, KT, D], F32R), at("wol", [P, KT, D], F32R)
        assert top[0] <= s_end
        top[0] = s_end
        p_base = top[0]
        tile_of = {n: at(n, [P, SW]) for n in KEPT}
        xb_base = p_base + 8 * 4 * SW
        nat_base = top[0]
        nat = [at(f"nat{i}", [P, NQ, P]) for i in range(2)]
        p_end = top[0]
        top[0] = xb_base
        xraw = [at(f"xraw{i}", [P, D]) for i in range(3)]
        g_pre = at("g_pre", [P, D])
        top[0] = nat_base
        xn = [at(f"xn{i}", [P, D]) for i in range(2)]
        top[0] = nat_base
        v_a = at("v_a", [P, NQ, W_BR])
        top[0] = p_base + 4 * 4 * SW
        v_c = at("v_c", [P, NQ, W_BR])
        top[0] = p_base + 4 * 4 * SW
        wo_raw = [at(f"wo_raw{i}", [P, D]) for i in range(4)]
        top[0] = xb_base
        y_sb = [at(f"y_sb{i}", [P, D]) for i in range(2)]
        x_res = [at(f"x_res{i}", [P, D]) for i in range(2)]
        top[0] = nat_base
        g_post = at("g_post", [P, D])
        top[0] = p_end
        us = at("us", [P, NT, NB])
        rows = [at(f"rows{i}", [NB, 4 * P]) for i in range(2)]
        bdiag = at("bdiag", [P, 4, 2, P])
        res_a, res_c = at("res_a", [P, NB, 24]), at("res_c", [P, NB, 12])
        sn_a, sn_c = at("sn_a", [P, NB, HCA]), at("sn_c", [P, NB, HC])
        mx_a, mx_c = at("mx_a", [P, NB, HCA]), at("mx_c", [P, NB, HC])
        m_a, m_c = at("m_a", [P, NB, HCA]), at("m_c", [P, NB, HC])
        ds_a, ds_c = at("ds_a", [P, NB, HCA]), at("ds_c", [P, NB, HC])
        sc_c = [at(f"sc_c{i}", [P, 3, HC]) for i in range(2)]
        ex_c = [at(f"ex_c{i}", [P, 3, HC]) for i in range(2)]
        snat = at("snat", [NB, 16])
        ident = at("ident", [P, P])
        ones = at("ones", [P, P])
        bones = at("bones", [P, P])
        sel = at("sel", [P, 16])
        pageT = at("pageT", [P, NB], I32)
        quarter = at("quarter", [P, 1])
        index = at("index", [P, NB], U32)
        pT = at("pT", [P, 4, 8])
        sT = at("sT", [P, 4, 4 * NB])
        tail = rows[0][0:3, :]
        lam2 = at("lam2", [P, 2])
        neglam = at("neglam", [P, 1])
        eps = at("eps", [P, 1])
        ss = at("ss", [P, 16])
        rstd = at("rstd", [P, 16])
        yss = at("yss", [P, 16])
        yrs = at("yrs", [P, 16])
        gsub = at("gsub", [P, 1])
        c4 = at("c4", [P, 4])
        nc4 = at("nc4", [P, 4])
        sp = at("sp", [P, 6, 4])
        hb = at("hb", [P, 4, 2])
        den = at("den", [P, 4, 2])
        rden = at("rden", [P, 4, 2])
        negmax = at("negmax", [P, 4])
        lamv, lamp = at("lamv", [P, 4, DKA]), at("lamp", [P, 2, DKA])
        top[0] -= 4 * 6 * DKA
        w1 = at("w1", [P, 12, 32])
        assert top[0] <= nc.sbuf_usable_end, (top[0], nc.sbuf_usable_end)

        ps = ctx.enter_context(nc.psum_tensor("ps", [P, 8, 512], F32))
        flat = ps[:].rearrange("p b n -> p (b n)")
        JB, RB, VB = 5, 6, 7

        gate_d = dram("gate_d", [len(GATES), P, SW])
        q_d = dram("q_d", [2, NB, W_BR])
        sn_d = dram("sn_d", [2, NB, HCA])

        x_d, xs_d = a["x_prompt"][0], a["x_sample"].rearrange("b t d -> (b t) d")
        w_in = a["w_in"][0].rearrange("(kt p) n -> p kt n", p=P)
        w_out = a["w_out"][0].rearrange("(kt p) n -> kt p n", p=P)
        ck = a["cache_a_k"].rearrange("l n (q r) h d -> (l n q) (r h d)", q=QPP)
        cv = a["cache_a_v"].rearrange("l n (q r) h d -> (l n q) (r h d)", q=QPP)
        cck = a["cache_c_k"][0].rearrange("b s h d -> b s (h d)")
        ccv = a["cache_c_v"][0].rearrange("b s h d -> b s (h d)")
        (y_p, y_s, ak_p, av_p, ak_s, av_s, cn_p, cn_s, lr_p, lr_s, ck_p, cv_p, ck_s, cv_s) = o
        y_p, y_s = y_p[0], y_s.rearrange("b t d -> (b t) d")
        nat_out = {n: t.rearrange("l b (s p) h d -> p (l b s) (h d)", p=P)
                   for n, t in (("ka", ak_p), ("va", av_p), ("kc", ck_p), ("vc", cv_p))}
        row_out = {n: t.rearrange("l b t h d -> (l b t) (h d)")
                   for n, t in (("ka", ak_s), ("va", av_s), ("kc", ck_s), ("vc", cv_s))}

        consts_in = sem("consts_in")
        late_in = sem("late_in")
        x_in = [sem(f"x_in{i}") for i in range(3)]
        w_landed = [sem(f"w_in{i}") for i in range(3)]
        k_in = [sem(f"k_in{i}") for i in range(2)]
        v_in = [sem(f"v_in{i}") for i in range(3)]
        q_in = [sem(f"q_in{i}") for i in range(2)]
        kc_in, qc_in = sem("kc_in"), sem("qc_in")
        vc_in = [sem(f"vc_in{i}") for i in range(2)]
        sn_in = [sem("sn_in0"), sem("sn_in1")]
        nat_out_done = [sem(f"nat_out{i}") for i in range(2)]
        rows_out = [sem(f"rows_out{i}") for i in range(2)]
        snat_out = sem("snat_out")
        q_out = sem("q_out")
        gate_out = [sem(f"gate_out{i}") for i in range(3)]
        gate_in = sem("gate_in")
        misc_out = sem("misc_out")
        stack_in = [sem(f"stack_in{i}") for i in range(2)]
        va_in, vc_nat_in = sem("va_in"), sem("vc_nat_in")
        wo_in = [sem(f"wo_in{i}") for i in range(4)]
        res_in = [sem(f"res_in{i}") for i in range(2)]
        gpost_in = sem("gpost_in")
        y_out = [sem(f"y_out{i}") for i in range(2)]

        setup_done = sem("setup_done")
        index_done = sem("index_done")
        first_in, pages_in = sem("first_in"), sem("pages_in")
        early, early_out = sem("early"), sem("early_out")
        squares = sem("squares")
        roots = sem("roots")
        xn_done = sem("xn_done")
        x_turned = sem("x_turned")
        xh_done, xl_done = sem("xh_done"), sem("xl_done")
        wh_done, wl_done = sem("wh_done"), sem("wl_done")
        proj = sem("proj")
        evac = sem("evac")
        gated = sem("gated")
        job = sem("job")
        job_out = sem("job_out")
        snat_done = sem("snat_done")
        k_used = sem("k_used")
        mx_done, m_done = sem("mx_done"), sem("m_done")
        sub_done, ex_done, ds_done = sem("sub_done"), sem("ex_done"), sem("ds_done")
        v_used = sem("v_used")
        acc_out = sem("acc_out")
        picked, res_done = sem("picked"), sem("res_done")
        kc_used, mxc_done, mc_done = sem("kc_used"), sem("mxc_done"), sem("mc_done")
        subc_done, exc_done, dsc_done = sem("subc_done"), sem("exc_done"), sem("dsc_done")
        picked_c, res_c_done = sem("picked_c"), sem("res_c_done")
        acc_zero = sem("acc_zero")
        split_done = sem("split_done")
        scored = sem("scored")
        score_read = sem("score_read")
        item_read = sem("item_read")
        exped = sem("exped")
        pd_done = sem("pd_done")
        turned = sem("turned")
        pt_out = sem("pt_out")
        attended, core_out = sem("attended"), sem("core_out")
        conv_done, lru_a, lru_om, lru_rt = sem("conv_done"), sem("lru_a"), sem("lru_om"), sem("lru_rt")
        lru_h, lru_mix = sem("lru_h"), sem("lru_mix")
        lru_xi = sem("lru_xi")
        sq_done, nrm_root, nrm_done = sem("sq_done"), sem("nrm_root"), sem("nrm_done")
        mix_c = sem("mix_c")
        smix = sem("smix")
        s_dve, s_act, s_pe = sem("s_dve"), sem("s_act"), sem("s_pe")
        mh_done, ml_done = sem("mh_done"), sem("ml_done")
        woh_done, wol_done = sem("woh_done"), sem("wol_done")
        y_done = sem("y_done")
        y_sq, y_rt, y_nrm, y_add = sem("y_sq"), sem("y_rt"), sem("y_nrm"), sem("y_add")
        dve_link, act_link, pool_link = sem("dve_link"), sem("act_link"), sem("pool_link")

        NCONST = 19
        X_ORDER = [NQ] + list(range(NQ))
        PAST = cck.shape[1]
        C_ROWS = [slice(PAST - 128, PAST), slice(PAST - 512, PAST, 4), slice(0, PAST, 16)]

        def bank_of(t, c):
            return (3 * t + c) % 5

        def kind(t):
            n = NAMES[t]
            return "gate" if n[0] == "g" else ("v" if n[0] == "v" else "kept")

        def gate_no(t, c):
            return 3 * sum(kind(i) == "gate" for i in range(t)) + c + 1

        def slot_of(name):
            return PASSING.index(name) % 3

        def passing_free(eng, name):
            i = PASSING.index(name)
            if i >= 3:
                before = PASSING[i - 3]
                if before[0] == "v":
                    eng.wait_ge(job, JOB_NO["turn", before, 1] + 1)
                else:
                    n = sum(slot_of(g) == slot_of(before) for g in GATES[:GATE_AT[before] + 1])
                    eng.wait_ge(gate_out[slot_of(before)], 16 * n)

        def dest(t):
            n = NAMES[t]
            return tile_of[n] if n in tile_of else passing[slot_of(n)]

        def stacked(hh):
            return 16 * sum(16 if x < HA else 6 for x in range(hh % 2, hh + 1, 2))

        def keep_free(eng, it):
            i = ITEM_NO[it]
            if i >= 2:
                b = ITEMS[i - 2]
                if b[0] == "s":
                    eng.wait_ge(score_read, SCORE_NO[b] + 1)
                else:
                    eng.wait_ge(item_read, OTHER_NO[b] + 1)

        def score_bank(it):
            return flat[:, (ITEM_NO[it] % 2) * S:(ITEM_NO[it] % 2 + 1) * S]

        ALL_CHUNKS = 3 * NT
        NGATE = 3 * len(GATES)

        def stage1_over(eng):
            eng.wait_ge(proj, ALL_CHUNKS)
            eng.wait_ge(evac, ALL_CHUNKS)
            eng.wait_ge(gated, NGATE)
            eng.wait_ge(job_out, len(JOBS))
            for i in range(3):
                eng.wait_ge(gate_out[i], 16 * sum(slot_of(g) == i for g in GATES))

        def a_tail(eng):
            eng.wait_ge(res_done, NB)
            eng.wait_ge(res_c_done, NB)

        block = ctx.enter_context(nc.Block())

        @block.sync
        def _(sp):
            n_const = [0]

            def load(dst, src, slow=False):
                sp.dma_start(dst, src, allow_slow_non_contiguous=slow).then_inc(consts_in, 16)
                n_const[0] += 1

            def load_x(i):
                if i >= 3:
                    sp.wait_ge(xn_done, i - 2)
                s = X_ORDER[i]
                src = x_d[s * P:(s + 1) * P, :] if s < NQ else xs_d
                n = P if s < NQ else NB
                sp.dma_start(xraw[i % 3][0:n, :], src).then_inc(x_in[i % 3], 16)

            def load_w(t):
                if t >= 3:
                    sp.wait_ge(wl_done, t - 2)
                c = TILES[t][1]
                sp.dma_start(wraw[t % 3][:], w_in[:, :, c:c + P]).then_inc(w_landed[t % 3], 16)

            pt = a["page_table"].rearrange("b j -> j b")
            load_x(0)
            sp.dma_start(ident[:], a["c_ident"]).then_inc(first_in, 16)
            sp.dma_start(g_pre[:], a["ln_pre"][0].partition_broadcast(P)).then_inc(first_in, 16)
            load_x(1)
            load_w(0)
            load_x(2)
            load_w(1)
            for q in range(QPP):
                sp.dma_start(pageT[q:q + QPP * (PAGES - 1) + 1:QPP, :], pt, allow_slow_non_contiguous=True)\
                  .then_inc(pages_in, 16)
            sp.dma_start(quarter[:], a["c_quarter"]).then_inc(pages_in, 16)
            for i in range(3, NQ + 1):
                load_x(i)
                if i == 6:
                    sp.wait_ge(early_out, 2)
                    sp.dma_start(q_d[0], rows[1][:, 0:W_BR]).then_inc(q_out, 16)
                    sp.wait_ge(q_out, 16)
                    for b in range(2):
                        sp.dma_start(qrep[b][:], q_d[0, b].partition_broadcast(P)).then_inc(q_in[b], 16)
            load_w(2)
            load(bones[:], a["c_bones"])
            load(sel[:], a["c_sel"])
            load(prow[0:4, :], a["conv_w"][0])
            load(prow[4:5, :], a["conv_b"])
            load(prow[5:6, :], a["b_rgate"])
            load(prow[6:7, :], a["b_igate"])
            load(prow[7:8, :], a["lru_lambda"])
            load(srow[0:24, :], a["state_conv"].rearrange("l b k d -> (l b k) d"))
            load(srow[24:32, :], a["state_lru"][0])
            for i, n in enumerate(("lam_q1", "lam_q2", "lam_k1", "lam_k2")):
                load(lamv[:, i, :], a[n][0].partition_broadcast(P))
            for r in range(2):
                load(gsub[64 * r:64 * r + 64, :], a["subln_g"].rearrange("l d -> d l"), slow=True)
            sp.wait_ge(setup_done, 1)
            for g, n in enumerate(("w_rgate", "w_igate")):
                w = a[n][0].rearrange("(f r) d e -> r d f e", r=2)
                for r in range(2):
                    load(bdiag[64 * r:64 * r + 64, :, g, 64 * r:64 * r + 64], w[r])
            assert n_const[0] == NCONST, n_const
            cs = cn_s[0]
            sp.dma_start(cs[:, 0:2, :], a["state_conv"][0][:, 1:3, :]).then_inc(misc_out, 16)

            turn_no = [0]
            for step in range(PSTEPS + 8):
                t, kt = divmod(step, KT)
                if kt == 0 and 1 <= t and t + 2 < NT:
                    load_w(t + 2)
                ji = JOB_AT.get(step - 1)
                if ji is not None:
                    _, k, arg, h = JOBS[ji]
                    if k == "turn" and h == 1:
                        sp.wait_ge(job_out, ji + 1)
                        i = turn_no[0] % 2
                        f = int(arg[2]) * P
                        sp.dma_start(nat_out[arg[:2]][:, :, f:f + P], nat[i][:]).then_inc(nat_out_done[i], 16)
                        turn_no[0] += 1
                    if k == "rows":
                        sp.wait_ge(job_out, ji + 1)
                        r = rows[arg % 2]
                        n = (("qa", "ka"), ("va", "vc"), ("qc", "kc"), None)[arg]
                        if n is None:
                            sp.dma_start(cs[:, 2, :], r[:]).then_inc(rows_out[1], 16)
                        else:
                            for i, m in enumerate(n):
                                if m == "qa":
                                    continue
                                dst = q_d[1] if m == "qc" else row_out[m]
                                sp.dma_start(dst, r[:, i * W_BR:(i + 1) * W_BR]).then_inc(rows_out[arg % 2], 16)
                        if arg in (0, 2):
                            e = arg // 2
                            w = (HCA, HC)[e]
                            sp.wait_ge(snat_done, e + 1)
                            sp.dma_start(sn_d[e, :, 0:w], snat[:, 8 * e:8 * e + w]).then_inc(snat_out, 16)
                            sp.wait_ge(snat_out, 16 * (e + 1))
                            sp.wait_ge(rows_out[0], (16, 48)[e])
                            dst = (sn_a, sn_c)[e]
                            sp.dma_start(dst[:], sn_d[e, :, 0:w].partition_broadcast(P)).then_inc(sn_in[e], 16)
                    if k == "tail":
                        sp.wait_ge(job_out, ji + 1)
                        sp.dma_start(cn_p[0, 0], tail).then_inc(misc_out, 16)
                n = K_AT.get(step - 1)
                if n is not None and n % NCH == NCH - 1 and 2 <= n // NCH + 2 < NB:
                    b = n // NCH + 2
                    sp.wait_ge(k_used, n + 1)
                    sp.dma_start(qrep[b % 2][:], q_d[0, b].partition_broadcast(P)).then_inc(q_in[b % 2], 16)
                b = C_STEP.get(step + 5)
                if b is not None:
                    if b >= 1:
                        sp.wait_ge(kc_used, b)
                    sp.dma_start(qrep_c[:], q_d[1, b].partition_broadcast(P)).then_inc(qc_in, 16)
                    for i, r in enumerate(C_ROWS):
                        sp.dma_start(kc[:, i, :], cck[b, r, :]).then_inc(kc_in, 16)
                    if b >= 2:
                        sp.wait_ge(job, JOB_NO["cpv", b - 2, 0] + 1)
                    for i, r in enumerate(C_ROWS):
                        sp.dma_start(vc[b % 2][:, i, :], ccv[b, r, :]).then_inc(vc_in[b % 2], 16)
                if kt == 1 and t >= 1 and t - 1 < NT and kind(t - 1) == "gate":
                    sp.wait_ge(gated, gate_no(t - 1, 2))
                    i = slot_of(NAMES[t - 1])
                    sp.dma_start(gate_d[GATE_AT[NAMES[t - 1]]], passing[i][:]).then_inc(gate_out[i], 16)

            stage1_over(sp)
            sp.dma_start(mask_a[:], a["c_mask_a"]).then_inc(late_in, 16)
            sp.dma_start(mask_c[:], a["c_mask_c"]).then_inc(late_in, 16)
            for i in range(2):
                sp.wait_ge(nat_out_done[i], 16 * 4)
            sp.dma_start(v_a[:], nat_out["va"]).then_inc(va_in, 16)

            def load_stack(hh):
                sl = stack[hh % 2]
                sp.wait_ge(split_done, 4 * (hh // 2 + 1))
                if hh >= 2:
                    last = UNITS.index((hh - 2, NQ - 1))
                    sp.wait_ge(scored, ITEM_NO["s", last, 1 if hh - 2 < HA else 0] + 1)
                if hh < HA:
                    for c in range(2):
                        r = 64 * (hh % 2) + 32 * c
                        for g in range(4):
                            q, k = (QH, QL)[g % 2], (KH, KL)[g // 2]
                            sp.dma_start(sl[2 * c][32 * g:32 * g + 32, :].bitcast(F32), q[r:r + 32, :].bitcast(F32))\
                              .then_inc(stack_in[hh % 2], 16)
                            sp.dma_start(sl[2 * c + 1][32 * g:32 * g + 32, :].bitcast(F32), k[r:r + 32, :].bitcast(F32))\
                              .then_inc(stack_in[hh % 2], 16)
                else:
                    r = 64 * (hh % 2)
                    for g in range(2):
                        for d, s_ in ((0, (QH, QL)[g]), (1, KH), (2, KL)):
                            sp.dma_start(sl[d][64 * g:64 * g + 64, :].bitcast(F32), s_[r:r + 64, :].bitcast(F32))\
                              .then_inc(stack_in[hh % 2], 16)

            load_stack(0)
            load_stack(1)
            n_gate = 0
            for u in range(NU + 1):
                h, q = UNITS[u] if u < NU else (8, 0)
                if q == 1 and h >= 1 and h + 1 < 8:
                    load_stack(h + 1)
                if u == UNITS.index((HA, 2)):
                    sp.wait_ge(stack_in[1], stacked(3))
                    sp.dma_start(v_c[:], nat_out["vc"]).then_inc(vc_nat_in, 16)
                if u - 3 in LRU_AT:
                    f = LRU_AT[u - 3]
                    sp.wait_ge(lru_h, f + 1)
                    sp.dma_start(TMP[1][:], gate_d[GATE_AT[f"gb{f}"]]).then_inc(gate_in, 16)
                    sp.dma_start(lr_p[0, 0, f * P:(f + 1) * P].unsqueeze(1), tile_of[f"xb{f}"][:, S - 1:S],
                                 allow_slow_non_contiguous=True)\
                      .then_inc(misc_out, 16)
                if u - 2 in NORM_AT:
                    p = NORM_AT[u - 2]
                    sp.wait_ge(sq_done, p + 1)
                    sp.dma_start(TMP[2][:], gate_d[GATE_AT[f"ga{p}"]]).then_inc(gate_in, 16)
            for p in range(2):
                if p == 0:
                    sp.wait_ge(nrm_done, 2)
                sp.dma_start(TMP[p][:], gate_d[GATE_AT[f"gc{p}"]]).then_inc(gate_in, 16)
            sp.wait_ge(attended, NU)
            sp.wait_ge(lru_mix, 4)

            def load_wo(k):
                if k >= 4:
                    sp.wait_ge(wol_done, k - 3)
                sp.dma_start(wo_raw[k % 4][:], w_out[k]).then_inc(wo_in[k % 4], 16)

            for k in range(4):
                load_wo(k)
            sp.dma_start(g_post[:], a["ln_post"][0].partition_broadcast(P)).then_inc(gpost_in, 16)
            for k in range(4, KT):
                load_wo(k)
            sp.wait_ge(ml_done, KT + 1)

            def load_res(s):
                if s >= 2:
                    sp.wait_ge(y_add, s - 1)
                src = x_d[s * P:(s + 1) * P, :] if s < NQ else xs_d
                sp.dma_start(x_res[s % 2][0:P if s < NQ else NB, :], src).then_inc(res_in[s % 2], 16)

            load_res(0)
            load_res(1)
            sp.wait_ge(smix, 1)
            for f in range(4):
                sp.dma_start(lr_s[0].rearrange("b (f p) -> f p b", p=P)[f], w1[:, 11, NB * f:NB * (f + 1)],
                             allow_slow_non_contiguous=True).then_inc(misc_out, 16)
            for s in range(NQ + 1):
                sp.wait_ge(y_add, s + 1)
                n = P if s < NQ else NB
                dst = y_p[s * P:(s + 1) * P, :] if s < NQ else y_s
                sp.dma_start(dst, y_sb[s % 2][0:n, :]).then_inc(y_out[s % 2], 16)
                if s + 2 <= NQ:
                    load_res(s + 2)
            sp.wait_ge(y_out[0], 16 * 5)
            sp.wait_ge(y_out[1], 16 * 4)
            sp.wait_ge(misc_out, 16 * 10)
            sp.wait_ge(rows_out[0], 48)
            sp.wait_ge(rows_out[1], 48)

        @block.gpsimd
        def _(pool):
            n_link = [0]

            def link(ins):
                n_link[0] += 1
                ins.then_inc(pool_link, 1)
                pool.wait_ge(pool_link, n_link[0])

            def split_w(t):
                pool.wait_ge(wh_done, t + 1)
                if t >= 2:
                    pool.wait_ge(proj, 3 * (t - 1))
                pool.tensor_tensor(wl[t % 2][:], wraw[t % 3][:], wh[t % 2][:].bitcast(F32), ALU.subtract)\
                    .then_inc(wl_done, 1)

            def load_k(n):
                if n >= 2:
                    pool.wait_ge(k_used, n - 1)
                b, c = divmod(n, NCH)
                pool.indirect_dma_start(kbuf[n % 2][:].rearrange("p s d -> p (s d)"), None, ck,
                                        bass.IndirectOffsetOnAxis(ap=index[:, b:b + 1], axis=0),
                                        element_offset=c * CH * W_BR).then_inc(k_in[n % 2], 16)

            def load_v(m):
                if m >= 3:
                    pool.wait_ge(v_used, m - 2)
                b, c = divmod(m, NCH)
                pool.indirect_dma_start(vbuf[m % 3][:].rearrange("p s d -> p (s d)"), None, cv,
                                        bass.IndirectOffsetOnAxis(ap=index[:, b:b + 1], axis=0),
                                        element_offset=c * CH * W_BR).then_inc(v_in[m % 3], 16)

            def sample_events(step):
                n = K_AT.get(step - 1)
                if n is not None:
                    if n + 2 < NK:
                        load_k(n + 2)
                if step - 1 in MAX_AT:
                    b = MAX_AT[step - 1]
                    pool.wait_ge(mx_done, b + 1)
                    pool.partition_all_reduce(m_a[:, b, :], mx_a[:, b, :], P, RMAX).then_inc(m_done, 1)
                m = V_AT.get(step - 1)
                if m is not None and m + 3 < NK:
                    load_v(m + 3)
                b = C_STEP.get(step - 1)
                if b is not None:
                    pool.wait_ge(mxc_done, b + 1)
                    pool.partition_all_reduce(m_c[:, b, :], mx_c[:, b, :], P, RMAX).then_inc(mc_done, 1)

            split_w(0)
            split_w(1)
            pool.wait_ge(index_done, 1)
            for n in range(2):
                load_k(n)
            for m in range(3):
                load_v(m)
            for step in range(PSTEPS):
                t, kt = divmod(step, KT)
                if kt == 0 and 1 <= t and t + 1 < NT:
                    split_w(t + 1)
                sample_events(step)
            stage1_over(pool)

            def split_pair(p):
                if p >= 1:
                    for i in range(2):
                        pool.wait_ge(stack_in[i], stacked(2 * (p - 1) + i))
                q, k = tile_of[("qa0", "qa1", "qc0", "qc1")[p]], tile_of[("ka0", "ka1", "kc0", "kc1")[p]]
                pool.tensor_copy(QH[:], q[:, 0:S]).then_inc(split_done, 1)
                pool.tensor_copy(KH[:], k[:, 0:S]).then_inc(split_done, 1)
                pool.wait_ge(split_done, 4 * p + 2)
                pool.tensor_tensor(QL[:], q[:, 0:S], QH[:].bitcast(F32), ALU.subtract).then_inc(split_done, 1)
                pool.tensor_tensor(KL[:], k[:, 0:S], KH[:].bitcast(F32), ALU.subtract).then_inc(split_done, 1)

            split_pair(0)
            for u in range(NU):
                h, q = UNITS[u]
                if q == 4 and h in (0, 2, 4):
                    split_pair(h // 2 + 1)
                sample_events(PSTEPS + 2 * u)
                sample_events(PSTEPS + 2 * u + 1)
            for k in range(KT):
                pool.wait_ge(woh_done, k + 1)
                pool.tensor_tensor(wol[:, k, :], wo_raw[k % 4][:], woh[:, k, :].bitcast(F32), ALU.subtract)\
                    .then_inc(wol_done, 1)
            for s in range(NQ + 1):
                n = P if s < NQ else NB
                pool.wait_ge(y_nrm, s + 1)
                pool.wait_ge(res_in[s % 2], 16 * (s // 2 + 1))
                pool.tensor_tensor(y_sb[s % 2][0:n, :], y_sb[s % 2][0:n, :], x_res[s % 2][0:n, :], ALU.add)\
                    .then_inc(y_add, 1)

        @block.scalar
        def _(act):
            n_link = [0]

            def link(ins):
                n_link[0] += 1
                ins.then_inc(act_link, 1)
                act.wait_ge(act_link, n_link[0])

            def split_w(t):
                act.wait_ge(w_landed[t % 3], 16 * (t // 3 + 1))
                if t >= 2:
                    act.wait_ge(proj, 3 * (t - 1))
                act.activation(wh[t % 2][:], wraw[t % 3][:], ACT.Copy).then_inc(wh_done, 1)

            def x_high(i):
                s = X_ORDER[i]
                w = P if s < NQ else NB
                for h in range(2):
                    u = 2 * i + h
                    act.wait_ge(x_turned, u + 1)
                    src = ps[:, u % 5, 0:4 * w].rearrange("p (k n) -> p k n", n=w)
                    act.activation(xh[:, 4 * h:4 * h + 4, s * P:s * P + w], src, ACT.Copy).then_inc(xh_done, 1)

            act.wait_ge(setup_done, 1)
            for i, s in enumerate(X_ORDER):
                n = P if s < NQ else NB
                act.wait_ge(x_in[i % 3], 16 * (i // 3 + 1))
                if i >= 2:
                    act.wait_ge(x_turned, 2 * (i - 1))
                act.activation(xn[i % 2][0:n, :], xraw[i % 3][0:n, :], ACT.Square, accum_out=ss[0:n, i:i + 1])\
                    .then_inc(squares, 1)
                act.wait_ge(squares, i + 1)
                act.activation(rstd[0:n, i:i + 1], ss[0:n, i:i + 1], ACT.Sqrt, bias=eps[0:n, 0:1], scale=1.0 / D)\
                    .then_inc(roots, 1)
                if i in (1, 2):
                    split_w(i - 1)
                if i >= 1:
                    x_high(i - 1)
                if i == 5:
                    act.wait_ge(early, 2)
                    act.activation(us[:, 0:2, :], ps[:, JB, 0:16].rearrange("p (t b) -> p t b", b=NB), ACT.Copy)\
                       .then_inc(early_out, 1)
                if i == 6:
                    act.wait_ge(early, 3)
                    act.activation(rows[1][:, 0:W_BR], ps[0:NB, JB, 0:W_BR], ACT.Copy).then_inc(early_out, 1)
            x_high(NQ)

            def evacuate(t):
                d, k = dest(t), kind(t)
                if k != "kept":
                    passing_free(act, NAMES[t])
                if t in (TI["xb0"], TI["xb1"], TI["xb2"], TI["xb3"]) or (t < 2):
                    act.wait_ge(xl_done, 18)
                for c in range(3):
                    act.wait_ge(proj, 3 * t + c + 1)
                    src = ps[:, bank_of(t, c), 0:CW]
                    ins = act.activation(d[:, c * CW:(c + 1) * CW], src, ACT.Tanh if k == "gate" else ACT.Copy,
                                         scale=0.5 if k == "gate" else 1.0)
                    if c == 2 and k != "gate" and t >= 2:
                        ins = act.activation(us[:, t, :], src[:, CW - NB:CW], ACT.Copy)
                    ins.then_inc(evac, 1)

            turn_no = [0]

            def job_evac(ji):
                _, k, arg, h = JOBS[ji]
                act.wait_ge(job, ji + 1)
                if k == "param":
                    ins = act.activation(pT[:], ps[:, JB, 0:32].rearrange("p (f n) -> p f n", n=8), ACT.Copy)
                elif k == "state":
                    ins = act.activation(sT[:], ps[:, JB, 0:128].rearrange("p (f n) -> p f n", n=32), ACT.Copy)
                elif k == "rows":
                    if arg >= 2:
                        act.wait_ge(rows_out[arg % 2], (16, 32)[arg % 2])
                        if arg == 2:
                            act.wait_ge(snat_done, 1)
                    if arg == 1:
                        act.wait_ge(q_out, 16)
                    ins = act.activation(rows[arg % 2][:], ps[0:NB, JB, :], ACT.Copy)
                elif k == "tail":
                    act.wait_ge(rows_out[0], 48)
                    act.wait_ge(snat_done, 2)
                    ins = act.activation(tail, ps[0:3, JB, :], ACT.Copy)
                elif k == "turn":
                    i = turn_no[0] // 2
                    if i >= 2:
                        act.wait_ge(nat_out_done[i % 2], 16 * (i // 2))
                    ins = act.activation(nat[i % 2][:, 4 * h:4 * h + 4, :],
                                         ps[:, JB, :].rearrange("p (k n) -> p k n", n=P), ACT.Copy)
                    turn_no[0] += 1
                elif k == "cpv":
                    act.wait_ge(acc_zero, 2)
                    if arg >= 1:
                        act.wait_ge(picked_c, arg)
                    for i in range(3):
                        ins = act.activation(acc_c[32 * i:32 * i + HC, :], ps[32 * i:32 * i + HC, JB, 0:W_BR], ACT.Copy)
                ins.then_inc(job_out, 1)

            def sample_events(step):
                if step - 2 in MAX_AT:
                    exp_a(MAX_AT[step - 2])
                m = V_AT.get(step - 1)
                if m is not None and m % NCH == NCH - 1:
                    b = m // NCH
                    act.wait_ge(v_used, m + 1)
                    act.wait_ge(acc_zero, 2)
                    if b >= 1:
                        act.wait_ge(picked, b)
                    for i in range(4):
                        ins = act.activation(acc[32 * i:32 * i + HCA, :],
                                             ps[32 * i:32 * i + HCA, VB, 0:W_BR], ACT.Copy)
                    ins.then_inc(acc_out, 1)
                if step in PICK_AT:
                    b = PICK_AT[step]
                    act.wait_ge(picked, b + 1)
                    act.activation(res_a[:, b, :], ps[:, RB, 0:24], ACT.Copy).then_inc(res_done, 1)
                b = C_STEP.get(step - 3)
                if b is not None:
                    act.wait_ge(subc_done, b + 1)
                    if b >= 2:
                        act.wait_ge(job, JOB_NO["cpv", b - 2, 0] + 1)
                        act.wait_ge(dsc_done, b - 1)
                    act.activation(ex_c[b % 2][:], sc_c[b % 2][:], ACT.Exp, scale=SCALE_C).then_inc(exc_done, 1)
                b = C_STEP.get(step - 8)
                if b is not None:
                    act.wait_ge(picked_c, b + 1)
                    act.activation(res_c[:, b, :], ps[:, RB, 32:44], ACT.Copy).then_inc(res_c_done, 1)

            def exp_a(b):
                act.wait_ge(sub_done, b + 1)
                if b >= 2:
                    act.wait_ge(v_used, NCH * (b - 1))
                    act.wait_ge(ds_done, b - 1)
                act.activation(ex[b % 2][:], sc[b % 2][:], ACT.Exp, scale=SCALE_A).then_inc(ex_done, 1)

            for step in range(PSTEPS + 8):
                t, kt = divmod(step, KT)
                if kt == 0:
                    if t >= 1:
                        evacuate(t - 1)
                    if 1 <= t and t + 1 < NT:
                        split_w(t + 1)
                    if t == 0:
                        act.wait_ge(s_dve, 1)
                        act.activation(lam2[:], lam2[:], ACT.Exp).then_inc(s_act, 1)
                    if t == 2:
                        act.wait_ge(s_dve, 3)
                        link(act.activation(sp[:, 0, :], pT[:, :, 7], ACT.Abs))
                        act.activation(sp[:, 1, :], sp[:, 0, :], ACT.Exp, scale=-1.0).then_inc(s_act, 1)
                        act.wait_ge(s_dve, 4)
                        act.activation(sp[:, 3, :], sp[:, 2, :], ACT.Ln).then_inc(s_act, 1)
                if step < PSTEPS:
                    sample_events(step)
                ji = JOB_AT.get(step)
                if ji is not None:
                    job_evac(ji)

            def exps(u):
                h, q = UNITS[u]
                w = (q + 1) * P
                for c in range(2 if h < HA else 1):
                    k = SCORE_NO["s", u, c]
                    e = (2 * u + c) % 4
                    act.wait_ge(score_read, k + 1)
                    if u >= 2:
                        act.wait_ge(pd_done, u - 1)
                        act.wait_ge(turned, GROUP_NO[u - 2, 1 if UNITS[u - 2][1] >= 4 else 0] + 1)
                    act.activation(E[e][:, 0:w], T[k % 2][:, 0:w], ACT.Exp, bias=negmax[:, k % 4:k % 4 + 1], scale=-1.0,
                                   accum_out=den[:, u % 4, c:c + 1]).then_inc(exped, 1)

            def pt_evac(u):
                h, q = UNITS[u]
                for g in range(2 if q >= 4 else 1):
                    nb = min(4, q + 1 - 4 * g)
                    i = GROUP_NO[u, g]
                    act.wait_ge(turned, i + 1)
                    if u >= 2:
                        act.wait_ge(attended, u - 1)
                    act.activation(PT[u % 2][:, 4 * g:4 * g + nb, :],
                                   ps[:, 4 + i % 2, 0:nb * P].rearrange("p (k n) -> p k n", n=P), ACT.Copy)\
                       .then_inc(pt_out, 1)

            def core_evac(u):
                h, q = UNITS[u]
                r = 64 * (h % 2)
                act.wait_ge(attended, u + 1)
                d = tile_of[("qa0", "qa1", "qc0", "qc1")[h // 2]]
                act.wait_ge(split_done, 4 * (h // 2 + 1))
                act.activation(d[r:r + 64, q * P:(q + 1) * P], ps[r:r + 64, RB, 128:256],
                               ACT.Copy).then_inc(core_out, 1)

            def lru_gates(f):
                for w in range(2):
                    it = ("gate", f, w)
                    act.wait_ge(scored, ITEM_NO[it] + 1)
                    if w == 0 and f >= 1:
                        act.wait_ge(lru_mix, f)
                    act.activation(TMP[1 + w][:, 0:S], score_bank(it), ACT.Tanh, bias=hb[:, f, w:w + 1], scale=0.5)\
                       .then_inc(item_read, 1)
                act.wait_ge(item_read, OTHER_NO["gate", f, 0] + 1)
                act.activation(TMP[3][:, 0:S], TMP[1][:, 0:S], ACT.Exp, bias=c4[:, f:f + 1], scale=c4[:, f:f + 1])\
                   .then_inc(lru_a, 1)
                act.wait_ge(lru_a, 3 * f + 1)
                act.activation(TMP[1][:, 0:S], TMP[1][:, 0:S], ACT.Tanh, bias=nc4[:, f:f + 1], scale=nc4[:, f:f + 1])\
                   .then_inc(lru_a, 1)
                act.activation(tile_of[f"xb{f}"][:, 0:S], TMP[3][:, 0:S], ACT.Square).then_inc(lru_a, 1)

            stage1_over(act)
            for u in range(NU + 2):
                if u < NU:
                    exps(u)
                if 1 <= u <= NU:
                    pt_evac(u - 1)
                if u >= 2:
                    core_evac(u - 2)
                if u < NU:
                    sample_events(PSTEPS + 2 * u)
                    sample_events(PSTEPS + 2 * u + 1)
                if u - 1 in LRU_AT:
                    lru_gates(LRU_AT[u - 1])
                if u - 2 in LRU_AT:
                    f = LRU_AT[u - 2]
                    act.wait_ge(lru_om, f + 1)
                    act.activation(TMP[1][:, 0:S], TMP[1][:, 0:S], ACT.Sqrt).then_inc(lru_rt, 1)
                if u - 1 in NORM_AT:
                    p = NORM_AT[u - 1]
                    act.wait_ge(scored, ITEM_NO["norm", p, 0] + 1)
                    act.activation(TMP[1][:, 0:S], score_bank(("norm", p, 0)), ACT.Sqrt, bias=eps[:, 0:1])\
                       .then_inc(item_read, 1)

            act.wait_ge(s_dve, 5)
            act.activation(w1[:, 0, :].rearrange("p (b h) -> p b h", h=HC), m_c[:], ACT.Exp, scale=SCALE_C)
            act.activation(ds_a[:], m_a[:], ACT.Exp, scale=SCALE_A).then_inc(s_act, 1)
            act.wait_ge(s_dve, 6)
            link(act.activation(w1[:, 2:4, :], w1[:, 2:4, :], ACT.Tanh, scale=0.5))
            act.nop().then_inc(s_act, 1)
            act.wait_ge(s_dve, 7)
            act.activation(w1[:, 4, :], w1[:, 2, :], ACT.Exp)
            act.activation(w1[:, 5, :], w1[:, 2, :], ACT.Tanh, scale=-1.0).then_inc(s_act, 1)
            act.wait_ge(s_dve, 8)
            act.activation(w1[:, 5, :], w1[:, 5, :], ACT.Sqrt).then_inc(s_act, 1)
            act.wait_ge(s_pe, 2)
            act.activation(w1[:, 9, 0:16], ps[:, RB, 64:80], ACT.Sqrt, bias=eps[:, 0:1]).then_inc(s_act, 1)

            act.wait_ge(attended, NU)
            a_tail(act)
            for k, n in enumerate(MIX):
                if n[0] == "x":
                    act.wait_ge(lru_mix, k - 1)
                elif n[1] == "a":
                    act.wait_ge(nrm_done, k + 1)
                else:
                    act.wait_ge(mix_c, k - 5)
                act.activation(mh[:, k, NB:SW], tile_of[n][:, 0:S], ACT.Copy).then_inc(mh_done, 1)
                act.wait_ge(wo_in[k % 4], 16 * (k // 4 + 1))
                act.activation(woh[:, k, :], wo_raw[k % 4][:], ACT.Copy).then_inc(woh_done, 1)
            act.wait_ge(smix, 1)
            act.activation(mh[:, :, 0:NB], w1[:, 6:8, :].rearrange("p a (k b) -> p (a k) b", b=NB), ACT.Copy)\
               .then_inc(mh_done, 1)
            for s in range(NQ + 1):
                n = P if s < NQ else NB
                src = flat[0:n, (s % 3) * D:(s % 3 + 1) * D]
                act.wait_ge(y_done, s + 1)
                if s >= 2:
                    act.wait_ge(y_out[s % 2], 16 * (s // 2))
                act.activation(y_sb[s % 2][0:n, :], src, ACT.Square, accum_out=yss[0:n, s:s + 1]).then_inc(y_sq, 1)
                act.wait_ge(y_sq, s + 1)
                act.activation(yrs[0:n, s:s + 1], yss[0:n, s:s + 1], ACT.Sqrt, bias=eps[0:n, 0:1], scale=1.0 / D)\
                   .then_inc(y_rt, 1)

        @block.vector
        def _(dve):
            n_link = [0]

            def link(ins):
                n_link[0] += 1
                ins.then_inc(dve_link, 1)
                dve.wait_ge(dve_link, n_link[0])

            dve.memset(eps[:], EPS)
            dve.memset(acc[:], 0.0)
            dve.memset(acc_c[:], 0.0).then_inc(acc_zero, 2)
            dve.memset(ones[:], 1.0)
            dve.memset(bdiag[:], 0.0).then_inc(setup_done, 1)

            def x_low(i):
                s = X_ORDER[i]
                w = P if s < NQ else NB
                for h in range(2):
                    u = 2 * i + h
                    dve.wait_ge(xh_done, u + 1)
                    src = ps[:, u % 5, 0:4 * w].rearrange("p (k n) -> p k n", n=w)
                    dve.tensor_tensor(xl[:, 4 * h:4 * h + 4, s * P:s * P + w], src,
                                      xh[:, 4 * h:4 * h + 4, s * P:s * P + w].bitcast(F32), ALU.subtract)\
                       .then_inc(xl_done, 1)

            dve.wait_ge(first_in, 32)
            for i, s in enumerate(X_ORDER):
                n = P if s < NQ else NB
                dve.wait_ge(roots, i + 1)
                link(dve.reciprocal(rstd[0:n, i:i + 1], rstd[0:n, i:i + 1]))
                dve.scalar_tensor_tensor(out=xn[i % 2][0:n, :], in0=xraw[i % 3][0:n, :], scalar=rstd[0:n, i:i + 1],
                                         in1=g_pre[0:n, :], op0=ALU.mult, op1=ALU.mult).then_inc(xn_done, 1)
                if i >= 1:
                    x_low(i - 1)
                if i == 2:
                    dve.wait_ge(pages_in, 16 * 5)
                    dve.tensor_scalar(index[:], pageT[:], float(QPP), quarter[:, 0:1], ALU.mult, ALU.add)\
                       .then_inc(index_done, 1)
            x_low(NQ)
            dve.wait_ge(consts_in, 16 * NCONST)
            link(dve.tensor_tensor(lamp[:], lamv[:, 0:2, :], lamv[:, 2:4, :], ALU.mult))
            dve.tensor_reduce(lam2[:], lamp[:], AX, ALU.add).then_inc(s_dve, 1)
            dve.wait_ge(s_act, 1)
            link(dve.tensor_tensor(neglam[:], lam2[:, 1:2], lam2[:, 0:1], ALU.subtract))
            dve.tensor_scalar(neglam[:], neglam[:], LAM_INIT, None, ALU.subtract).then_inc(s_dve, 1)

            def gate_chunks(t):
                d = passing[slot_of(NAMES[t])]
                for c in range(3):
                    dve.wait_ge(evac, 3 * t + c + 1)
                    src = ps[:, bank_of(t, c), 0:CW]
                    part = d[:, c * CW:(c + 1) * CW]
                    if c == 2:
                        link(dve.scalar_tensor_tensor(out=us[:, t, :], in0=part[:, CW - NB:CW], scalar=1.0,
                                                      in1=src[:, CW - NB:CW], op0=ALU.add, op1=ALU.mult))
                    dve.scalar_tensor_tensor(out=part, in0=part, scalar=1.0, in1=src, op0=ALU.add, op1=ALU.mult)\
                       .then_inc(gated, 1)

            def new_scores(e):
                w, d = ((HCA, DKA), (HC, DHC))[e]
                dve.wait_ge(job_out, JOB_NO["rows", 2 * e, 0] + 1)
                r = rows[0]
                tmp = prod[0:NB, 0, :]
                if k_done[0]:
                    dve.wait_ge(k_used, k_done[0])
                link(dve.tensor_tensor(tmp, r[:, 0:W_BR], r[:, W_BR:2 * W_BR], ALU.mult))
                dve.tensor_reduce(snat[:, 8 * e:8 * e + w], tmp.rearrange("p (h d) -> p h d", d=d), AX, ALU.add)\
                   .then_inc(snat_done, 1)
                dve.wait_ge(snat_done, e + 1)

            k_done = [0]

            def k_chunk(n):
                b, c = divmod(n, NCH)
                dve.wait_ge(k_in[n % 2], 16 * (n // 2 + 1))
                if c == 0:
                    dve.wait_ge(q_in[b % 2], 16 * (b // 2 + 1))
                if n >= 1:
                    dve.wait_ge(k_used, n)
                if c == 0 and b >= 2:
                    dve.wait_ge(ex_done, b - 1)
                link(dve.tensor_tensor(prod[:], kbuf[n % 2][:], qrep[b % 2][:].unsqueeze(1).to_broadcast([P, CH, W_BR]),
                                       ALU.mult))
                dve.tensor_reduce(sc[b % 2][:, CH * c:CH * (c + 1), :],
                                  prod[:].rearrange("p s (h d) -> p s h d", d=DKA), AX, ALU.add).then_inc(k_used, 1)
                k_done[0] = n + 1

            def row_max(b):
                dve.wait_ge(sn_in[0], 16)
                dve.wait_ge(k_used, NCH * (b + 1))
                link(dve.tensor_reduce(mx_a[:, b, :], sc[b % 2][:].rearrange("p s h -> p h s"), AX, ALU.max))
                dve.tensor_tensor(mx_a[:, b, :], mx_a[:, b, :], sn_a[:, b, :], ALU.max).then_inc(mx_done, 1)

            def subtract_max(b):
                dve.wait_ge(m_done, b + 1)
                dve.tensor_tensor(sc[b % 2][:], sc[b % 2][:], m_a[:, b, :].unsqueeze(1).to_broadcast([P, PPP, HCA]),
                                  ALU.subtract).then_inc(sub_done, 1)

            def sum_exps(b):
                dve.wait_ge(ex_done, b + 1)
                dve.tensor_reduce(ds_a[:, b, :], ex[b % 2][:].rearrange("p s h -> p h s"), AX, ALU.add)\
                   .then_inc(ds_done, 1)

            def c_scores(b):
                dve.wait_ge(kc_in, 48 * (b + 1))
                dve.wait_ge(qc_in, 16 * (b + 1))
                if b == 0:
                    dve.wait_ge(sn_in[1], 16)
                if k_done[0]:
                    dve.wait_ge(k_used, k_done[0])
                if b >= 2:
                    dve.wait_ge(exc_done, b - 1)
                link(dve.tensor_tensor(prod[:, 0:3, :], kc[:], qrep_c[:].unsqueeze(1).to_broadcast([P, 3, W_BR]), ALU.mult))
                dve.tensor_reduce(sc_c[b % 2][:], prod[:, 0:3, :].rearrange("p s (h d) -> p s h d", d=DHC), AX, ALU.add)\
                   .then_inc(kc_used, 1)
                dve.wait_ge(kc_used, b + 1)
                link(dve.tensor_reduce(mx_c[:, b, :], sc_c[b % 2][:].rearrange("p s h -> p h s"), AX, ALU.max))
                dve.tensor_tensor(mx_c[:, b, :], mx_c[:, b, :], sn_c[:, b, :], ALU.max).then_inc(mxc_done, 1)

            def sample_events(step):
                n = K_AT.get(step)
                if n is not None:
                    k_chunk(n)
                b = C_STEP.get(step)
                if b is not None:
                    c_scores(b)
                if step in MAX_AT:
                    row_max(MAX_AT[step])
                if step - 2 in MAX_AT:
                    subtract_max(MAX_AT[step - 2])
                if step - 4 in MAX_AT:
                    sum_exps(MAX_AT[step - 4])
                b = C_STEP.get(step - 2)
                if b is not None:
                    dve.wait_ge(mc_done, b + 1)
                    dve.tensor_tensor(sc_c[b % 2][:], sc_c[b % 2][:], m_c[:, b, :].unsqueeze(1).to_broadcast([P, 3, HC]),
                                      ALU.subtract).then_inc(subc_done, 1)
                b = C_STEP.get(step - 4)
                if b is not None:
                    dve.wait_ge(exc_done, b + 1)
                    dve.tensor_reduce(ds_c[:, b, :], ex_c[b % 2][:].rearrange("p s h -> p h s"), AX, ALU.add)\
                       .then_inc(dsc_done, 1)

            for step in range(PSTEPS + 8):
                t, kt = divmod(step, KT)
                if kt == 0 and 1 <= t and kind(t - 1) == "gate":
                    gate_chunks(t - 1)
                if step < PSTEPS:
                    sample_events(step)
                ji = JOB_AT.get(step)
                if ji is not None and JOBS[ji][1] == "rows" and JOBS[ji][2] in (0, 2):
                    new_scores(JOBS[ji][2] // 2)
                if step == 2 * KT - 1:
                    dve.wait_ge(job_out, JOB_NO["param", 0, 0] + 1)
                    dve.tensor_scalar(hb[:], pT[:, :, 5:7], 0.5, None, ALU.mult).then_inc(s_dve, 1)
                    dve.wait_ge(s_act, 2)
                    e, w = sp[:, 1, :], sp[:, 2, :]
                    dve.tensor_scalar(w, e, 1.0, None, ALU.add).then_inc(s_dve, 1)
                    dve.wait_ge(s_act, 3)
                    link(dve.tensor_scalar(sp[:, 4, :], w, 1.0, None, ALU.is_equal))
                    link(dve.scalar_tensor_tensor(out=sp[:, 5, :], in0=w, scalar=-1.0, in1=sp[:, 4, :], op0=ALU.add,
                                                  op1=ALU.add))
                    link(dve.reciprocal(sp[:, 5, :], sp[:, 5, :]))
                    link(dve.tensor_tensor(sp[:, 4, :], sp[:, 3, :], sp[:, 4, :], ALU.add))
                    link(dve.tensor_tensor(sp[:, 4, :], sp[:, 4, :], sp[:, 5, :], ALU.mult))
                    link(dve.tensor_tensor(sp[:, 4, :], sp[:, 4, :], e, ALU.mult))
                    link(dve.tensor_scalar(sp[:, 5, :], pT[:, :, 7], -1.0, 0.0, ALU.mult, ALU.max))
                    link(dve.tensor_tensor(sp[:, 4, :], sp[:, 4, :], sp[:, 5, :], ALU.add))
                    dve.tensor_scalar(c4[:], sp[:, 4, :], -4.0, None, ALU.mult)
                    link(dve.tensor_scalar(nc4[:], sp[:, 4, :], 4.0, None, ALU.mult))

            stage1_over(dve)
            dve.wait_ge(late_in, 32)

            def mask_scores(u):
                h, q = UNITS[u]
                w = (q + 1) * P
                scale, mask = (SCALE_A, mask_a) if h < HA else (SCALE_C, mask_c)
                for c in range(2 if h < HA else 1):
                    it = ("s", u, c)
                    k = SCORE_NO[it]
                    dve.wait_ge(scored, ITEM_NO[it] + 1)
                    if k >= 2:
                        dve.wait_ge(exped, k - 1)
                    dve.tensor_tensor_reduce(T[k % 2][:, 0:w], score_bank(it)[:, 0:w], mask[:, S - w:S], -scale, 3.0e38,
                                             ALU.add, ALU.min, negmax[:, k % 4:k % 4 + 1]).then_inc(score_read, 1)

            def probs(u):
                h, q = UNITS[u]
                w = (q + 1) * P
                n = 2 if h < HA else 1
                e0, e1 = E[2 * u % 4], E[(2 * u + 1) % 4]
                d, r = den[:, u % 4, 0:n], rden[:, u % 4, 0:n]
                dve.wait_ge(exped, SCORE_NO["s", u, n - 1] + 1)
                link(dve.reciprocal(r, d))
                if h < HA:
                    link(dve.tensor_scalar(e1[:, 0:w], e1[:, 0:w], rden[:, u % 4, 1:2], neglam[:, 0:1], ALU.mult, ALU.mult))
                    dve.scalar_tensor_tensor(out=e0[:, 0:w], in0=e0[:, 0:w], scalar=rden[:, u % 4, 0:1], in1=e1[:, 0:w],
                                             op0=ALU.mult, op1=ALU.add).then_inc(pd_done, 1)
                else:
                    dve.tensor_scalar(e0[:, 0:w], e0[:, 0:w], rden[:, u % 4, 0:1], None, ALU.mult).then_inc(pd_done, 1)

            def conv(f):
                x, y = tile_of[f"xb{f}"], TMP[0]
                if f >= 1:
                    dve.wait_ge(lru_xi, f)
                    dve.wait_ge(scored, ITEM_NO["gate", f - 1, 1] + 1)
                link(dve.tensor_scalar(y[:, 0:S], x[:, 0:S], pT[:, f, 3:4], pT[:, f, 4:5], ALU.mult, ALU.add))
                for d in (1, 2):
                    link(dve.scalar_tensor_tensor(out=y[:, d:S], in0=x[:, 0:S - d], scalar=pT[:, f, 3 - d:4 - d],
                                                  in1=y[:, d:S], op0=ALU.mult, op1=ALU.add))
                dve.scalar_tensor_tensor(out=y[:, 3:S], in0=x[:, 0:S - 3], scalar=pT[:, f, 0:1], in1=y[:, 3:S],
                                         op0=ALU.mult, op1=ALU.add).then_inc(conv_done, 1)

            n_gate = [0]

            def gate_arrived():
                n_gate[0] += 1
                dve.wait_ge(gate_in, 16 * n_gate[0])

            for u in range(NU + 1):
                if u < NU:
                    mask_scores(u)
                if u >= 1:
                    probs(u - 1)
                if u < NU:
                    sample_events(PSTEPS + 2 * u)
                    sample_events(PSTEPS + 2 * u + 1)
                if u in LRU_AT:
                    conv(LRU_AT[u])
                if u - 2 in LRU_AT:
                    f = LRU_AT[u - 2]
                    dve.wait_ge(lru_a, 3 * f + 3)
                    dve.scalar_tensor_tensor(out=TMP[1][:, 0:S], in0=tile_of[f"xb{f}"][:, 0:S], scalar=1.0,
                                             in1=TMP[1][:, 0:S], op0=ALU.add, op1=ALU.mult).then_inc(lru_om, 1)
                    dve.scalar_tensor_tensor(out=TMP[2][:, 0:S], in0=TMP[2][:, 0:S], scalar=1.0, in1=TMP[0][:, 0:S],
                                             op0=ALU.add, op1=ALU.mult).then_inc(lru_xi, 1)
                    dve.wait_ge(lru_xi, f + 1)
                    dve.wait_ge(lru_rt, f + 1)
                    link(dve.scalar_tensor_tensor(out=TMP[2][:, 0:S], in0=TMP[2][:, 0:S], scalar=0.5, in1=TMP[1][:, 0:S],
                                                  op0=ALU.mult, op1=ALU.mult))
                    dve.tensor_tensor_scan(tile_of[f"xb{f}"][:, 0:S], TMP[3][:, 0:S], TMP[2][:, 0:S], 0.0,
                                           ALU.mult, ALU.add).then_inc(lru_h, 1)
                if u - 5 in LRU_AT:
                    f = LRU_AT[u - 5]
                    h = tile_of[f"xb{f}"]
                    gate_arrived()
                    dve.wait_ge(misc_out, 16 * (f + 3))
                    dve.scalar_tensor_tensor(out=h[:, 0:S], in0=h[:, 0:S], scalar=0.5, in1=TMP[1][:, 0:S],
                                             op0=ALU.mult, op1=ALU.mult).then_inc(lru_mix, 1)
                if u in NORM_AT:
                    p = NORM_AT[u]
                    t = tile_of[f"qa{p}"]
                    dve.wait_ge(core_out, 2 * NQ * (p + 1))
                    dve.wait_ge(lru_mix, 4)
                    if p:
                        dve.wait_ge(nrm_done, 1)
                    dve.tensor_tensor(TMP[0][:, 0:S], t[:, 0:S], t[:, 0:S], ALU.mult).then_inc(sq_done, 1)
                if u - 4 in NORM_AT:
                    p = NORM_AT[u - 4]
                    t = tile_of[f"qa{p}"]
                    dve.wait_ge(item_read, OTHER_NO["norm", p, 0] + 1)
                    link(dve.reciprocal(TMP[1][:, 0:S], TMP[1][:, 0:S]))
                    link(dve.scalar_tensor_tensor(out=TMP[1][:, 0:S], in0=TMP[1][:, 0:S], scalar=gsub[:, 0:1],
                                                  in1=t[:, 0:S], op0=ALU.mult, op1=ALU.mult))
                    gate_arrived()
                    dve.scalar_tensor_tensor(out=t[:, 0:S], in0=TMP[1][:, 0:S], scalar=0.5 * (1.0 - LAM_INIT),
                                             in1=TMP[2][:, 0:S], op0=ALU.mult, op1=ALU.mult).then_inc(nrm_done, 1)

            a_tail(dve)
            r3 = lambda i, n, m: w1[:, i, 0:n * m].rearrange("p (a b) -> p a b", b=m)
            dve.tensor_tensor(m_c[:], sn_c[:], m_c[:], ALU.subtract)
            dve.tensor_tensor(m_a[:], sn_a[:], m_a[:], ALU.subtract).then_inc(s_dve, 1)
            x = us[:, TI["xb0"]:TI["xb0"] + 4, :]
            st = sT[:, :, 0:24].rearrange("p f (b k) -> p f b k", k=3)
            h0 = sT[:, :, 24:32]

            def par(i):
                return pT[:, :, i:i + 1].to_broadcast([P, 4, NB])

            y, z = r3(1, 4, NB), r3(8, 4, NB)
            link(dve.tensor_tensor(y, x, par(3), ALU.mult))
            link(dve.tensor_tensor(y, y, par(4), ALU.add))
            for i in range(3):
                link(dve.tensor_tensor(z, st[:, :, :, i], par(i), ALU.mult))
                link(dve.tensor_tensor(y, y, z, ALU.add))
            dve.nop().then_inc(conv_done, 1)
            dve.wait_ge(s_pe, 1)
            for g in range(2):
                link(dve.tensor_tensor(r3(2 + g, 4, NB), ps[:, RB, 64 + 32 * g:96 + 32 * g].rearrange("p (f b) -> p f b", b=NB),
                                       par(5 + g), ALU.add))
            dve.nop().then_inc(s_dve, 1)
            dve.wait_ge(s_act, 5)
            link(dve.tensor_scalar(w1[:, 2:4, :], w1[:, 2:4, :], 1.0, None, ALU.add))
            link(dve.tensor_tensor(r3(2, 4, NB), r3(2, 4, NB), c4[:].unsqueeze(2).to_broadcast([P, 4, NB]), ALU.mult))
            dve.nop().then_inc(s_dve, 1)
            link(dve.scalar_tensor_tensor(out=w1[:, 3, :], in0=w1[:, 3, :], scalar=0.5, in1=w1[:, 1, :],
                                          op0=ALU.mult, op1=ALU.mult))
            dve.wait_ge(s_act, 6)
            link(dve.tensor_tensor(w1[:, 9, :], w1[:, 4, :], w1[:, 4, :], ALU.mult))
            dve.scalar_tensor_tensor(out=w1[:, 5, :], in0=w1[:, 9, :], scalar=1.0, in1=w1[:, 5, :],
                                     op0=ALU.add, op1=ALU.mult).then_inc(s_dve, 1)
            dve.wait_ge(s_act, 7)
            link(dve.tensor_tensor(w1[:, 3, :], w1[:, 3, :], w1[:, 5, :], ALU.mult))
            link(dve.tensor_tensor(r3(4, 4, NB), r3(4, 4, NB), h0, ALU.mult))
            link(dve.tensor_tensor(w1[:, 11, :], w1[:, 3, :], w1[:, 4, :], ALU.add))
            mix = w1[:, 6:8, :].rearrange("p a (k b) -> p (a k) b", b=NB)
            link(dve.scalar_tensor_tensor(out=mix[:, 2:6, :], in0=r3(11, 4, NB), scalar=0.5,
                                          in1=us[:, TI["gb0"]:TI["gb0"] + 4, :], op0=ALU.mult, op1=ALU.mult))
            dve.wait_ge(s_act, 4)
            num, dn, en = (w1[:, i, :].rearrange("p (j b c) -> p j b c", j=2, c=2) for i in (1, 2, 3))
            for j in range(2):
                for r in range(2):
                    hd, rw = 2 * j + r, slice(64 * r, 64 * r + 64)
                    dve.tensor_copy(num[rw, j], res_a[rw, :, 8 * j + 2 * hd:8 * j + 2 * hd + 2])
                    dve.tensor_copy(dn[rw, j], res_a[rw, :, 16 + 2 * hd:18 + 2 * hd])
                    link(dve.tensor_copy(en[rw, j], ds_a[rw, :, 2 * hd:2 * hd + 2]))
            link(dve.tensor_tensor(w1[:, 2, :], w1[:, 2, :], w1[:, 3, :], ALU.add))
            link(dve.tensor_tensor(en, en, us[:, TI["va0"]:TI["va0"] + 2, :].unsqueeze(3).to_broadcast([P, 2, NB, 2]),
                                   ALU.mult))
            link(dve.tensor_tensor(w1[:, 1, :], w1[:, 1, :], w1[:, 3, :], ALU.add))
            link(dve.reciprocal(w1[:, 2, :], w1[:, 2, :]))
            link(dve.tensor_tensor(w1[:, 1, :], w1[:, 1, :], w1[:, 2, :], ALU.mult))
            oa = r3(3, 2, NB)
            link(dve.scalar_tensor_tensor(out=oa, in0=num[:, :, :, 1], scalar=neglam[:, 0:1], in1=num[:, :, :, 0],
                                          op0=ALU.mult, op1=ALU.add))
            dve.tensor_tensor(w1[:, 8, 0:16], w1[:, 3, 0:16], w1[:, 3, 0:16], ALU.mult).then_inc(s_dve, 1)
            dve.wait_ge(s_act, 8)
            link(dve.reciprocal(w1[:, 9, 0:16], w1[:, 9, 0:16]))
            link(dve.scalar_tensor_tensor(out=w1[:, 3, 0:16], in0=w1[:, 3, 0:16], scalar=gsub[:, 0:1], in1=w1[:, 9, 0:16],
                                          op0=ALU.mult, op1=ALU.mult))
            link(dve.scalar_tensor_tensor(out=mix[:, 0:2, :], in0=oa, scalar=0.5 * (1.0 - LAM_INIT),
                                          in1=us[:, TI["ga0"]:TI["ga0"] + 2, :], op0=ALU.mult, op1=ALU.mult))
            link(dve.tensor_scalar(w1[:, 0, :], w1[:, 0, :], 3.0, None, ALU.mult))
            e_c = w1[:, 0, :].rearrange("p (b h) -> p b h", h=HC)
            num, dn, en = (r3(i, 2, NB) for i in (1, 2, 4))
            for j in range(2):
                for r in range(2):
                    hd, rw = 2 * j + r, slice(64 * r, 64 * r + 64)
                    dve.tensor_copy(num[rw, j], res_c[rw, :, 4 * j + hd])
                    dve.tensor_copy(dn[rw, j], res_c[rw, :, 8 + hd])
                    link(dve.tensor_copy(en[rw, j], e_c[rw, :, hd]))
            link(dve.tensor_tensor(dn, dn, en, ALU.add))
            link(dve.tensor_tensor(en, en, us[:, TI["vc0"]:TI["vc0"] + 2, :], ALU.mult))
            link(dve.tensor_tensor(num, num, en, ALU.add))
            link(dve.reciprocal(dn, dn))
            link(dve.tensor_tensor(num, num, dn, ALU.mult))
            dve.scalar_tensor_tensor(out=mix[:, 6:8, :], in0=num, scalar=0.5, in1=us[:, TI["gc0"]:TI["gc0"] + 2, :],
                                     op0=ALU.mult, op1=ALU.mult).then_inc(smix, 1)
            for p in range(2):
                t = tile_of[f"qc{p}"]
                if p == 0:
                    dve.wait_ge(core_out, NU)
                gate_arrived() if p else dve.wait_ge(gate_in, 16 * 8)
                dve.scalar_tensor_tensor(out=t[:, 0:S], in0=t[:, 0:S], scalar=0.5, in1=TMP[p][:, 0:S],
                                         op0=ALU.mult, op1=ALU.mult).then_inc(mix_c, 1)

            for k, n in enumerate(MIX):
                dve.wait_ge(mh_done, k + 1)
                if k == 6:
                    dve.wait_ge(mix_c, 2)
                dve.tensor_tensor(ml[:, k, NB:SW], tile_of[n][:, 0:S], mh[:, k, NB:SW].bitcast(F32), ALU.subtract)\
                   .then_inc(ml_done, 1)
            dve.wait_ge(mh_done, KT + 1)
            dve.wait_ge(smix, 1)
            dve.tensor_tensor(ml[:, :, 0:NB], mix, mh[:, :, 0:NB].bitcast(F32), ALU.subtract).then_inc(ml_done, 1)
            dve.wait_ge(gpost_in, 16)
            for s in range(NQ + 1):
                n = P if s < NQ else NB
                src = flat[0:n, (s % 3) * D:(s % 3 + 1) * D]
                dve.wait_ge(y_rt, s + 1)
                link(dve.reciprocal(yrs[0:n, s:s + 1], yrs[0:n, s:s + 1]))
                dve.scalar_tensor_tensor(out=y_sb[s % 2][0:n, :], in0=src, scalar=yrs[0:n, s:s + 1], in1=g_post[0:n, :],
                                         op0=ALU.mult, op1=ALU.mult).then_inc(y_nrm, 1)

        @block.tensor
        def _(pe):
            pe.wait_ge(first_in, 32)

            def early_q(t):
                pe.wait_ge(wl_done, t + 1)
                pe.wait_ge(xl_done, 2)
                out = ps[:, JB, NB * t:NB * (t + 1)]
                for kt in range(KT):
                    pe.matmul(out, wh[t][:, kt, :], xh[:, kt, S:SW], start=(kt == 0), stop=False)
                    pe.matmul(out, wh[t][:, kt, :], xl[:, kt, S:SW], start=False, stop=False)
                    ins = pe.matmul(out, wl[t][:, kt, :], xh[:, kt, S:SW], start=False, stop=(kt == KT - 1))
                ins.then_inc(early, 1)

            for i, s in enumerate(X_ORDER):
                n = P if s < NQ else NB
                pe.wait_ge(xn_done, i + 1)
                for h in range(2):
                    u = 2 * i + h
                    if u >= 5:
                        pe.wait_ge(xl_done, u - 4)
                    for k in range(4):
                        f = (4 * h + k) * P
                        ins = pe.transpose(ps[:, u % 5, k * n:(k + 1) * n], xn[i % 2][0:n, f:f + P], ident[0:n, 0:n])
                    ins.then_inc(x_turned, 1)
                if i in (2, 4):
                    early_q(i // 2 - 1)
                if i == 6:
                    pe.wait_ge(early_out, 1)
                    for t in range(2):
                        ins = pe.transpose(ps[0:NB, JB, t * P:(t + 1) * P], us[:, t, :], ident[:])
                    ins.then_inc(early, 1)
            pe.wait_ge(early_out, 2)
            pe.wait_ge(consts_in, 16 * NCONST)

            def job_pe(ji):
                _, k, arg, h = JOBS[ji]
                if ji >= 1:
                    pe.wait_ge(job_out, ji)
                if k == "param":
                    for f in range(4):
                        ins = pe.transpose(ps[:, JB, 8 * f:8 * f + 8], prow[:, f * P:(f + 1) * P], ident[0:8, 0:8])
                elif k == "state":
                    for f in range(4):
                        ins = pe.transpose(ps[:, JB, 32 * f:32 * f + 32], srow[:, f * P:(f + 1) * P], ident[0:32, 0:32])
                elif k == "rows":
                    pe.wait_ge(evac, 3 * (4 * arg + 4))
                    for i in range(4):
                        ins = pe.transpose(ps[0:NB, JB, i * P:(i + 1) * P], us[:, 4 * arg + i, :], ident[:])
                elif k == "tail":
                    for f in range(4):
                        ins = pe.transpose(ps[0:3, JB, f * P:(f + 1) * P], tile_of[f"xb{f}"][:, S - 3:S], ident[:])
                elif k == "turn":
                    t = TI[arg]
                    pe.wait_ge(evac, 3 * (t + 1))
                    for i in range(4):
                        c = (4 * h + i) * P
                        ins = pe.transpose(ps[:, JB, i * P:(i + 1) * P], dest(t)[:, c:c + P], ident[:])
                elif k == "cpv":
                    b = arg
                    pe.wait_ge(exc_done, b + 1)
                    pe.wait_ge(vc_in[b % 2], 48 * (b // 2 + 1))
                    for i in range(3):
                        ins = pe.matmul(ps[32 * i:32 * i + HC, JB, 0:W_BR], ex_c[b % 2][:, i, :], vc[b % 2][:, i, :],
                                        start=True, stop=True)
                ins.then_inc(job, 1)

            in_rb = [0, 0, 0]

            def results_free():
                for s_, n_ in zip((core_out, res_done, res_c_done), in_rb):
                    if n_:
                        pe.wait_ge(s_, n_)

            def pick_c(b):
                pe.wait_ge(job_out, JOB_NO["cpv", b, 0] + 1)
                results_free()
                in_rb[2] += 1
                pe.wait_ge(dsc_done, b + 1)
                for j in range(2):
                    pe.matmul(ps[:, RB, 32 + 4 * j:36 + 4 * j], acc_c[:, j * P:(j + 1) * P], sel[:, 8:12], start=True, stop=True)
                pe.matmul(ps[:, RB, 40:44], ones[:], ds_c[:, b, :], start=True, stop=True).then_inc(picked_c, 1)

            def pick(b):
                pe.wait_ge(acc_out, b + 1)
                results_free()
                in_rb[1] += 1
                pe.wait_ge(ds_done, b + 1)
                for j in range(2):
                    pe.matmul(ps[:, RB, 8 * j:8 * j + 8], acc[:, j * P:(j + 1) * P], sel[:, 0:8], start=True, stop=True)
                pe.matmul(ps[:, RB, 16:24], ones[:], ds_a[:, b, :], start=True, stop=True).then_inc(picked, 1)

            def sample_events(step):
                m = V_AT.get(step)
                if m is not None:
                    b, c = divmod(m, NCH)
                    pe.wait_ge(v_in[m % 3], 16 * (m // 3 + 1))
                    if c == 0:
                        pe.wait_ge(ex_done, b + 1)
                        if b >= 1:
                            pe.wait_ge(acc_out, b)
                    for i in range(CH):
                        o_ = ps[32 * i:32 * i + HCA, VB, 0:W_BR]
                        ins = pe.matmul(o_, ex[b % 2][:, CH * c + i, :], vbuf[m % 3][:, i, :],
                                        start=(c == 0), stop=(c == NCH - 1))
                    ins.then_inc(v_used, 1)
                if step in PICK_AT:
                    pick(PICK_AT[step])
                b = C_STEP.get(step - 8)
                if b is not None:
                    pick_c(b)

            for step in range(PSTEPS):
                t, kt = divmod(step, KT)
                if kt == 0:
                    pe.wait_ge(wl_done, t + 1)
                    if t == 0:
                        pe.wait_ge(xl_done, 18)
                for c in range(3):
                    if kt == 0 and 3 * t + c >= 5:
                        bt, bc = divmod(3 * t + c - 5, 3)
                        if kind(bt) == "gate":
                            pe.wait_ge(gated, gate_no(bt, bc))
                        else:
                            pe.wait_ge(evac, 3 * bt + bc + 1)
                    pr = ps[:, bank_of(t, c), 0:CW]
                    cols = slice(c * CW, (c + 1) * CW)
                    pe.matmul(pr, wh[t % 2][:, kt, :], xh[:, kt, cols], start=(kt == 0), stop=False)
                    pe.matmul(pr, wh[t % 2][:, kt, :], xl[:, kt, cols], start=False, stop=False)
                    ins = pe.matmul(pr, wl[t % 2][:, kt, :], xh[:, kt, cols], start=False, stop=(kt == KT - 1))
                    if kt == KT - 1:
                        ins.then_inc(proj, 1)
                sample_events(step)
                ji = JOB_AT.get(step)
                if ji is not None:
                    job_pe(ji)

            stage1_over(pe)

            def scores(u):
                h, q = UNITS[u]
                w = (q + 1) * P
                sl = stack[h % 2]
                if q == 0:
                    pe.wait_ge(stack_in[h % 2], stacked(h))
                for c in range(2 if h < HA else 1):
                    it = ("s", u, c)
                    keep_free(pe, it)
                    out = score_bank(it)
                    for k0 in range(0, w, 512):
                        k1 = min(w, k0 + 512)
                        if h < HA:
                            ins = pe.matmul(out[:, k0:k1], sl[2 * c][:, q * P:(q + 1) * P], sl[2 * c + 1][:, k0:k1],
                                            start=True, stop=True)
                        else:
                            pe.matmul(out[:, k0:k1], sl[0][:, q * P:(q + 1) * P], sl[1][:, k0:k1], start=True, stop=False)
                            ins = pe.matmul(out[:, k0:k1], sl[0][:, q * P:(q + 1) * P], sl[2][:, k0:k1],
                                            start=False, stop=True)
                    ins.then_inc(scored, 1)

            def turn(u):
                h, q = UNITS[u]
                pe.wait_ge(pd_done, u + 1)
                for g in range(2 if q >= 4 else 1):
                    i = GROUP_NO[u, g]
                    if i >= 2:
                        pe.wait_ge(pt_out, i - 1)
                    for k in range(min(4, q + 1 - 4 * g)):
                        c = (4 * g + k) * P
                        ins = pe.transpose(ps[:, 4 + i % 2, k * P:(k + 1) * P], E[2 * u % 4][:, c:c + P], ident[:])
                    ins.then_inc(turned, 1)

            def attend(u):
                h, q = UNITS[u]
                r = 64 * (h % 2)
                pe.wait_ge(pt_out, GROUP_NO[u, 1 if q >= 4 else 0] + 1)
                results_free()
                in_rb[0] += 1
                if u == 0:
                    pe.wait_ge(va_in, 16)
                if h == HA and q == 0:
                    pe.wait_ge(vc_nat_in, 16)
                v = v_a if h < HA else v_c
                f = (h % 4) * 64
                for k in range(q + 1):
                    ins = pe.matmul(ps[r:r + 64, RB, 128:256], v[:, k, f:f + 64],
                                    PT[u % 2][:, k, :], start=(k == 0), stop=(k == q))
                ins.then_inc(attended, 1)

            for u in range(-1, NU + 2):
                if u + 1 < NU:
                    scores(u + 1)
                if u - 1 in LRU_AT:
                    f = LRU_AT[u - 1]
                    pe.wait_ge(conv_done, f + 1)
                    for w in range(2):
                        it = ("gate", f, w)
                        keep_free(pe, it)
                        for k0 in (0, 512):
                            ins = pe.matmul(score_bank(it)[:, k0:k0 + 512], bdiag[:, f, w, :], TMP[0][:, k0:k0 + 512],
                                            start=True, stop=True)
                        ins.then_inc(scored, 1)
                if u - 1 in NORM_AT:
                    it = ("norm", NORM_AT[u - 1], 0)
                    pe.wait_ge(sq_done, NORM_AT[u - 1] + 1)
                    keep_free(pe, it)
                    for k0 in (0, 512):
                        ins = pe.matmul(score_bank(it)[:, k0:k0 + 512], bones[:], TMP[0][:, k0:k0 + 512],
                                        start=True, stop=True)
                    ins.then_inc(scored, 1)
                if 1 <= u <= NU:
                    turn(u - 1)
                if u >= 2:
                    attend(u - 2)
                if 0 <= u < NU:
                    sample_events(PSTEPS + 2 * u)
                    sample_events(PSTEPS + 2 * u + 1)

            a_tail(pe)
            results_free()
            pe.wait_ge(conv_done, 5)
            for g in range(2):
                for f in range(4):
                    ins = pe.matmul(ps[:, RB, 64 + 32 * g + 8 * f:72 + 32 * g + 8 * f], bdiag[:, f, g, :],
                                    w1[:, 1, 8 * f:8 * f + 8], start=True, stop=True)
            ins.then_inc(s_pe, 1)
            pe.wait_ge(s_dve, 9)
            pe.matmul(ps[:, RB, 64:80], bones[:], w1[:, 8, 0:16], start=True, stop=True).then_inc(s_pe, 1)

            pe.wait_ge(ml_done, KT + 1)
            pe.wait_ge(core_out, NU)
            pe.wait_ge(s_act, 8)
            for s in range(NQ + 1):
                cols = slice(NB + s * P, NB + (s + 1) * P) if s < NQ else slice(0, P)
                if s >= 3:
                    pe.wait_ge(y_nrm, s - 2)
                for k in range(KT):
                    if s == 0:
                        pe.wait_ge(wol_done, k + 1)
                    for n in range(2):
                        out = flat[:, (s % 3) * D + n * 512:(s % 3) * D + (n + 1) * 512]
                        w_ = slice(n * 512, (n + 1) * 512)
                        pe.matmul(out, mh[:, k, cols], woh[:, k, w_], start=(k == 0), stop=False)
                        pe.matmul(out, mh[:, k, cols], wol[:, k, w_], start=False, stop=False)
                        ins = pe.matmul(out, ml[:, k, cols], woh[:, k, w_], start=False, stop=(k == KT - 1))
                ins.then_inc(y_done, 1)


_INS = ["x_prompt", "x_sample", "cache_a_k", "cache_a_v", "state_conv", "state_lru", "cache_c_k", "cache_c_v",
        "page_table", "ln_pre", "ln_post", "w_in", "w_out", "lam_q1", "lam_k1", "lam_q2", "lam_k2", "subln_g",
        "conv_w", "conv_b", "w_rgate", "b_rgate", "w_igate", "b_igate", "lru_lambda"]
_OUTS = [(1, S, D), (NB, 1, D), (1, 1, S, HA, 64), (1, 1, S, HA, 64), (1, NB, 1, HA, 64), (1, NB, 1, HA, 64),
         (1, 1, 3, DL), (1, NB, 3, DL), (1, 1, DL), (1, NB, DL), (1, 1, S, HC, DHC), (1, 1, S, HC, DHC),
         (1, NB, 1, HC, DHC), (1, NB, 1, HC, DHC)]


def _constants():
    import numpy as np

    i, j = np.arange(P)[:, None], np.arange(P)[None, :]
    mask_a = np.zeros((P, S), np.float32)
    mask_a[:, S - P:] = np.where(j <= i, 0.0, NEG)
    mask_c = np.zeros((P, S), np.float32)
    for b in range(NQ):
        dist = P * (NQ - 1 - b) + i - j
        count = sum(((dist >= 0) & (dist <= win) & (dist % dil == 0)).astype(int)
                    for win, dil in ((128, 1), (512, 4), (2048, 16)))
        mask_c[:, b * P:(b + 1) * P] = np.where(count > 0, np.log(np.maximum(count, 1)) / SCALE_C, NEG)
    sel = np.zeros((P, 16), np.float32)
    for q in range(4):
        for h in range(HCA):
            sel[32 * q + h, h] = 1.0
        for h in range(HC):
            if q < 3:
                sel[32 * q + h, 8 + h] = 1.0
    return {"c_ident": np.eye(P, dtype=np.float32), "c_bones": np.where(i // 64 == j // 64, 1.0 / 64, 0.0).astype(np.float32),
            "c_sel": sel, "c_mask_a": mask_a, "c_mask_c": mask_c.astype(np.float32),
            "c_quarter": (np.arange(P) % QPP).astype(np.float32).reshape(P, 1)}


def kernel(**inputs):
    import numpy as np
    import concourse.bacc as bacc
    from concourse.bass_utils import run_bass_kernel_spmd

    nc = bacc.Bacc("TRN2", target_bir_lowering=False, num_devices=1, dynamic_dma_scratch_size=4096)
    arrays, aps = {}, {}
    given = {n: np.ascontiguousarray(inputs[n]) for n in _INS}
    for name, arr in {**given, **_constants()}.items():
        arrays[f"in_{name}"] = arr
        aps[name] = nc.dram_tensor(f"in_{name}", arr.shape, mybir.dt.from_np(arr.dtype), kind="ExternalInput").ap()
    outs = [nc.dram_tensor(f"out_{i}", list(s), F32, kind="ExternalOutput").ap() for i, s in enumerate(_OUTS)]
    build(nc, aps, outs)
    r = run_bass_kernel_spmd(nc, [arrays], core_ids=[0])
    return tuple(r.results[0][f"out_{i}"] for i in range(len(_OUTS)))
```

```python
from contextlib import ExitStack

import concourse.bass as bass
from concourse import mybir

P = 128
S = 1024
NB = 8
SW = S + NB
D = 1024
KT = D // P
HA, DKA = 4, 32
HC, DHC = 4, 64
HCA = 2 * HA
W_BR = 256
DL = 512
PAGES, PAGE = 32, 128
QPP = P // PAGES
PPP = PAGE // QPP
CH = 4
NCH = PPP // CH
NK = NB * NCH
SCALE_A, SCALE_C = DKA ** -0.5, DHC ** -0.5
EPS = 1e-6
LAM_INIT = 0.2
NEG = -1.0e30
CW = SW // 3

F32, F32R = mybir.dt.float32, mybir.dt.float32r
I32, U32 = mybir.dt.int32, mybir.dt.uint32
ALU = mybir.AluOpType
ACT = mybir.ActivationFunctionType
AX = mybir.AxisListType.X
RMAX = bass.bass_isa.ReduceOp.max

TILES = [("qa0", 0), ("qa1", 128), ("ka0", 256), ("ka1", 384), ("va0", 512), ("va1", 640),
         ("vc0", 2560), ("vc1", 2688), ("qc0", 2048), ("qc1", 2176), ("kc0", 2304), ("kc1", 2432),
         ("xb0", 1024), ("xb1", 1152), ("xb2", 1280), ("xb3", 1408),
         ("gb0", 1536), ("gb1", 1664), ("gb2", 1792), ("gb3", 1920),
         ("ga0", 768), ("ga1", 896), ("gc0", 2816), ("gc1", 2944)]
NAMES = [n for n, _ in TILES]
NT = len(TILES)
TI = {n: t for t, n in enumerate(NAMES)}
KEPT = ["qa0", "qa1", "qc0", "qc1", "ka0", "ka1", "kc0", "kc1", "xb0", "xb1", "xb2", "xb3"]
PASSING = [n for n in NAMES if n not in KEPT]
GATES = [n for n in NAMES if n[0] == "g"]
GATE_AT = {n: i for i, n in enumerate(GATES)}
MIX = ["qa0", "qa1", "xb0", "xb1", "xb2", "xb3", "qc0", "qc1"]


def mix_scale(n):
    return {"qa": 1.0, "qc": 0.5, "xb": 0.25}[n[:2]]


PSTEPS = NT * KT
K_FIRST, V_LAG = 1, 16


def k_step(n):
    return K_FIRST + 3 * n


def v_step(m):
    return k_step(m + V_LAG)


K_AT = {k_step(n): n for n in range(NK)}
V_AT = {v_step(m): m for m in range(NK)}
MAX_AT = {max(k_step(NCH * b + NCH - 1), 36 + b): b for b in range(NB)}
assert all(v_step(NCH * b) >= s + 3 for s, b in MAX_AT.items())
PICK_AT = {v_step(NCH * b + NCH - 1) + 4: b for b in range(NB)}
C_STEP = {(13 + b) * KT: b for b in range(NB)}

JOBS = [(8 * 1 + 2, "param", 0, 0), (8 * 1 + 5, "state", 0, 0),
        (8 * 4 + 1, "rows", 0, 0), (8 * 8 + 1, "rows", 1, 0), (8 * 12 + 1, "rows", 2, 0),
        (8 * 16 + 1, "rows", 3, 0), (8 * 16 + 3, "tail", 0, 0)]
for _n in ("ka0", "ka1", "va0", "va1", "vc0", "vc1", "kc0", "kc1"):
    for _h in range(2):
        JOBS.append((8 * (TI[_n] + 1) + 3 + 3 * _h, "turn", _n, _h))
for _s, _b in C_STEP.items():
    JOBS.append((_s + 7, "cpv", _b, 0))
SPLIT_AT = [(NT - 7) * KT + 3, (NT - 6) * KT + 3, (NT - 3) * KT + 3, (NT - 3) * KT + 6]
JOBS.sort()
JOB_NO = {(k, a, h): i for i, (_, k, a, h) in enumerate(JOBS)}
JOB_AT = {s: i for i, (s, _, _, _) in enumerate(JOBS)}
TURNS = [j for j in JOBS if j[1] == "turn"]
assert len(JOB_AT) == len(JOBS)

NQ = S // P
UNITS = [(h, q) for h in range(HA + HC) for q in range(NQ)]
NU = len(UNITS)
LRU_AT = {1 + 11 * f: f for f in range(4)}
NORM_AT = {47: 0, 55: 1}
MIX_C_AT = 52
SAMPLE_AT = 34
WO_AT = {41 + k: k for k in range(KT)}
YS_AT = {51 + i + i // 4: i for i in range(8)}
assert PSTEPS + 2 * SAMPLE_AT > max(PICK_AT) and SAMPLE_AT + 15 < min(YS_AT)

ITEMS = []
for _u in range(-1, NU):
    if _u + 1 < NU:
        ITEMS += [("s", _u + 1, c) for c in range(2 if UNITS[_u + 1][0] < HA else 1)]
    for _i in range(4):
        if _u - 2 - _i in LRU_AT:
            ITEMS += [("gate", LRU_AT[_u - 2 - _i], _i)]
    if _u - 2 in NORM_AT:
        ITEMS += [("norm", NORM_AT[_u - 2], 0)]
ITEM_NO = {it: i for i, it in enumerate(ITEMS)}
NS_BEFORE = [sum(x[0] == "s" for x in ITEMS[:i + 1]) for i in range(len(ITEMS))]
SCORE_NO = {it: NS_BEFORE[i] - 1 for it, i in ITEM_NO.items() if it[0] == "s"}
OTHER_NO = {it: i - NS_BEFORE[i] for it, i in ITEM_NO.items() if it[0] != "s"}
GROUPS = [(u, g) for u, (h, q) in enumerate(UNITS) for g in range(2 if q >= 4 else 1)]
GROUP_NO = {x: i for i, x in enumerate(GROUPS)}


def build(nc, a, o):
    with ExitStack() as ctx:
        def sem(name):
            return ctx.enter_context(nc.semaphore(name))

        top = [0]

        def at(name, shape, dt=F32):
            size = 4
            for n in shape[1:]:
                size *= n
            size = -(-size // 32) * 32
            t = nc.alloc_sbuf_tensor_at(name, shape, dt, offset=top[0])
            top[0] += size
            return t

        def dram(name, shape):
            return nc.dram_tensor(name, shape, F32, kind="Internal").ap()

        base = -(-nc.sbuf_base // 32) * 32
        top[0] = base
        xh, xl = at("xh", [P, KT, SW], F32R), at("xl", [P, KT, SW], F32R)
        x_end = top[0]
        top[0] = base
        stack = [[at(f"stack{s}{i}", [P, S], F32R) for i in range(4)] for s in range(2)]
        E = [at(f"E{i}", [P, S]) for i in range(4)]
        T = [at(f"T{i}", [P, S]) for i in range(2)]
        PT = [at(f"PT{i}", [P, NQ, P]) for i in range(2)]
        assert top[0] <= x_end
        top[0] = base
        mh, ml = at("mh", [P, KT, SW], F32R), at("ml", [P, KT, SW], F32R)
        w_base = x_end
        top[0] = w_base
        wraw = [at(f"wraw{i}", [P, KT, P]) for i in range(3)]
        wh = [at(f"wh{i}", [P, KT, P], F32R) for i in range(2)]
        wl = [at(f"wl{i}", [P, KT, P], F32R) for i in range(2)]
        passing = [at(f"passing{i}", [P, SW]) for i in range(3)]
        w_end = top[0]
        top[0] = w_base
        mask_a, mask_c = at("mask_a", [P, S]), at("mask_c", [P, S])
        TMP = [at(f"TMP{i}", [P, SW]) for i in range(4)]
        v_base = top[0]
        v_a = at("v_a", [P, NQ, W_BR])
        wo = [at("wo0", [P, 2, D], F32R)]
        w_end = max(w_end, top[0])
        top[0] = w_end
        s_base = top[0]
        kbuf = [at(f"kbuf{i}", [P, CH, W_BR]) for i in range(2)]
        vbuf = [at(f"vbuf{i}", [P, CH, W_BR]) for i in range(3)]
        prod = at("prod", [P, CH, W_BR])
        s_mid = top[0]
        sc = [at(f"sc{i}", [P, PPP, HCA]) for i in range(2)]
        ex = [at(f"ex{i}", [P, PPP, HCA]) for i in range(2)]
        qrep = [at(f"qrep{i}", [P, W_BR]) for i in range(2)]
        acc = at("acc", [P, W_BR])
        acc_c = at("acc_c", [P, W_BR])
        qrep_c = at("qrep_c", [P, W_BR])
        prow, srow = at("prow", [NB, DL]), at("srow", [4 * NB, DL])
        top[0] -= 4 * 2 * DL
        kc = at("kc", [P, 3, W_BR])
        vc = [at(f"vc{i}", [P, 3, W_BR]) for i in range(2)]
        s_end = top[0]
        top[0] = s_base
        wo += [at(f"wo{k}", [P, 2, D], F32R) for k in (1, 2, 3)]
        assert top[0] == s_mid
        wo.append(at("wo4", [P, 2, D], F32R))
        k_base = s_end - 2 * 4 * S
        sxh, sxl = at("sxh", [P, KT, NB], F32R), at("sxl", [P, KT, NB], F32R)
        assert top[0] <= k_base
        top[0] = k_base
        KH, KL = at("KH", [P, S], F32R), at("KL", [P, S], F32R)
        top[0] = v_base
        wo.append(at("wo5", [P, 2, D], F32R))
        top[0] = k_base
        wo.append(at("wo6", [P, 2, D], F32R))
        top[0] = s_end
        p_base = top[0]
        tile_of = {n: at(n, [P, SW]) for n in KEPT}
        xb_base = p_base + 8 * 4 * SW
        nat_base = top[0]
        nat = [at(f"nat{i}", [P, NQ, P]) for i in range(2)]
        p_end = top[0]
        top[0] = xb_base
        xraw = [at(f"xraw{i}", [P, D]) for i in range(3)]
        g_pre = at("g_pre", [P, D])
        top[0] = nat_base
        xn = [at(f"xn{i}", [P, D]) for i in range(2)]
        top[0] = nat_base
        QH, QL = at("QH", [P, S], F32R), at("QL", [P, S], F32R)
        assert top[0] <= p_end
        top[0] = nat_base
        wo.append(at("wo7", [P, 2, D], F32R))
        top[0] = p_base + 4 * 4 * SW
        v_c = at("v_c", [P, NQ, W_BR])
        wo_raw = [tile_of[f"kc{i}"][:, 0:D] for i in range(2)]
        top[0] = xb_base
        y_sb = [at(f"y_sb{i}", [P, D]) for i in range(2)]
        x_res = [at(f"x_res{i}", [P, D]) for i in range(2)]
        top[0] = v_base - 4 * SW
        g_post = at("g_post", [P, D])
        top[0] = p_end
        us = at("us", [P, NT, NB])
        rows = [at(f"rows{i}", [NB, 4 * P]) for i in range(2)]
        top[0] -= 2 * 4 * 4 * P
        ys_raw = at("ys_raw", [NB, D])
        bdiag = at("bdiag", [P, 4, 2, P])
        res_a, res_c = at("res_a", [P, NB, 24]), at("res_c", [P, NB, 12])
        sn_a, sn_c = at("sn_a", [P, NB, HCA]), at("sn_c", [P, NB, HC])
        mx_a, mx_c = at("mx_a", [P, NB, HCA]), at("mx_c", [P, NB, HC])
        m_a, m_c = at("m_a", [P, NB, HCA]), at("m_c", [P, NB, HC])
        ds_a, ds_c = at("ds_a", [P, NB, HCA]), at("ds_c", [P, NB, HC])
        sc_c = [at(f"sc_c{i}", [P, 3, HC]) for i in range(2)]
        ex_c = [at(f"ex_c{i}", [P, 3, HC]) for i in range(2)]
        snat = at("snat", [NB, 16])
        ident = at("ident", [P, P])
        ones = at("ones", [P, P])
        bones = at("bones", [P, P])
        sel = at("sel", [P, 16])
        pageT = at("pageT", [P, NB], I32)
        quarter = at("quarter", [P, 1])
        index = at("index", [P, NB], U32)
        pT = at("pT", [P, 4, 8])
        sT = at("sT", [P, 4, 4 * NB])
        tail = rows[0][0:3, :]
        lam2 = at("lam2", [P, 2])
        neglam = at("neglam", [P, 1])
        eps = at("eps", [P, 1])
        ss = at("ss", [P, 16])
        rstd = at("rstd", [P, 16])
        yss = at("yss", [P, 16])
        yrs = at("yrs", [P, 16])
        gsub = at("gsub", [P, 1])
        c4 = at("c4", [P, 4])
        nc4 = at("nc4", [P, 4])
        sp = at("sp", [P, 6, 4])
        hb = at("hb", [P, 4, 2])
        den = at("den", [P, 4, 2])
        rden = at("rden", [P, 4, 2])
        negmax = at("negmax", [P, 4])
        lamv, lamp = at("lamv", [P, 4, DKA]), at("lamp", [P, 2, DKA])
        top[0] -= 4 * 6 * DKA
        w1 = at("w1", [P, 12, 32])
        assert top[0] <= nc.sbuf_usable_end, (top[0], nc.sbuf_usable_end)

        ps = ctx.enter_context(nc.psum_tensor("ps", [P, 8, 512], F32))
        flat = ps[:].rearrange("p b n -> p (b n)")
        JB, RB, VB = 5, 6, 7

        gate_d = dram("gate_d", [len(GATES), P, SW])
        q_d = dram("q_d", [2, NB, W_BR])
        sn_d = dram("sn_d", [2, NB, HCA])
        qa_d, ka_d = dram("qa_d", [2, 4, 2, DKA, S]), dram("ka_d", [2, 4, 4, DKA, S])
        qc_d, kc_d = dram("qc_d", [2, 2, 2, DHC, S]), dram("kc_d", [2, 2, P, S])

        x_d, xs_d = a["x_prompt"][0], a["x_sample"].rearrange("b t d -> (b t) d")
        w_in = a["w_in"][0].rearrange("(kt p) n -> p kt n", p=P)
        w_out = a["w_out"][0].rearrange("(kt p) n -> kt p n", p=P)
        ck = a["cache_a_k"].rearrange("l n (q r) h d -> (l n q) (r h d)", q=QPP)
        cv = a["cache_a_v"].rearrange("l n (q r) h d -> (l n q) (r h d)", q=QPP)
        cck = a["cache_c_k"][0].rearrange("b s h d -> b s (h d)")
        ccv = a["cache_c_v"][0].rearrange("b s h d -> b s (h d)")
        (y_p, y_s, ak_p, av_p, ak_s, av_s, cn_p, cn_s, lr_p, lr_s, ck_p, cv_p, ck_s, cv_s) = o
        y_p, y_s = y_p[0], y_s.rearrange("b t d -> (b t) d")
        nat_out = {n: t.rearrange("l b (s p) h d -> p (l b s) (h d)", p=P)
                   for n, t in (("ka", ak_p), ("va", av_p), ("kc", ck_p), ("vc", cv_p))}
        row_out = {n: t.rearrange("l b t h d -> (l b t) (h d)")
                   for n, t in (("ka", ak_s), ("va", av_s), ("kc", ck_s), ("vc", cv_s))}

        consts_in = sem("consts_in")
        mask_in = sem("mask_in")
        late_in = sem("late_in")
        x_in = [sem(f"x_in{i}") for i in range(3)]
        w_landed = [sem(f"w_in{i}") for i in range(3)]
        k_in = [sem(f"k_in{i}") for i in range(2)]
        v_in = [sem(f"v_in{i}") for i in range(3)]
        q_in = [sem(f"q_in{i}") for i in range(2)]
        kc_in, qc_in = sem("kc_in"), sem("qc_in")
        vc_in = [sem(f"vc_in{i}") for i in range(2)]
        sn_in = [sem("sn_in0"), sem("sn_in1")]
        nat_out_done = [sem(f"nat_out{i}") for i in range(2)]
        rows_out = [sem(f"rows_out{i}") for i in range(2)]
        snat_out = sem("snat_out")
        q_out = sem("q_out")
        gate_out = [sem(f"gate_out{i}") for i in range(3)]
        gate_in, norm_gate_in = sem("gate_in"), sem("norm_gate_in")
        c_gate_in = [sem(f"c_gate_in{i}") for i in range(2)]
        misc_out = sem("misc_out")
        qk_out = sem("qk_out")
        first_stack = sem("first_stack")
        stack_in = [sem(f"stack_in{i}") for i in range(2)]
        va_in, vc_nat_in = sem("va_in"), sem("vc_nat_in")
        wo_in = [sem(f"wo_in{i}") for i in range(2)]
        res_in = [sem(f"res_in{i}") for i in range(2)]
        gpost_in = sem("gpost_in")
        y_out = [sem(f"y_out{i}") for i in range(2)]

        setup_done = sem("setup_done")
        index_done = sem("index_done")
        first_in, pages_in = sem("first_in"), sem("pages_in")
        early, early_out = sem("early"), sem("early_out")
        squares = sem("squares")
        roots = sem("roots")
        xn_done = sem("xn_done")
        x_turned = sem("x_turned")
        xh_done, xl_done = sem("xh_done"), sem("xl_done")
        wh_done, wl_done = sem("wh_done"), sem("wl_done")
        proj = sem("proj")
        evac = sem("evac")
        gated = sem("gated")
        job = sem("job")
        job_out = sem("job_out")
        snat_done = sem("snat_done")
        k_used = sem("k_used")
        mx_done, m_done = sem("mx_done"), sem("m_done")
        sub_done, ex_done, ds_done = sem("sub_done"), sem("ex_done"), sem("ds_done")
        v_used = sem("v_used")
        acc_out = sem("acc_out")
        picked, res_done = sem("picked"), sem("res_done")
        kc_used, mxc_done, mc_done = sem("kc_used"), sem("mxc_done"), sem("mc_done")
        subc_done, exc_done, dsc_done = sem("subc_done"), sem("exc_done"), sem("dsc_done")
        picked_c, res_c_done = sem("picked_c"), sem("res_c_done")
        acc_zero = sem("acc_zero")
        split_done = sem("split_done")
        scored = sem("scored")
        score_read = sem("score_read")
        item_read = sem("item_read")
        exped = sem("exped")
        pd_done = sem("pd_done")
        turned = sem("turned")
        pt_out = sem("pt_out")
        attended, core_out = sem("attended"), sem("core_out")
        conv_done, lru_a, lru_om, lru_rt = sem("conv_done"), sem("lru_a"), sem("lru_om"), sem("lru_rt")
        lru_h, lru_mix = sem("lru_h"), sem("lru_mix")
        lru_sq = sem("lru_sq")
        lru_xi, lru_in, lru_last = sem("lru_xi"), sem("lru_in"), sem("lru_last")
        sq_done, nrm_done = sem("sq_done"), sem("nrm_done")
        mix_c = sem("mix_c")
        smix = sem("smix")
        tail_out = sem("tail_out")
        s_conv, ys_part = sem("s_conv"), sem("ys_part")
        sxh_done, sxl_done, ys_out = sem("sxh_done"), sem("sxl_done"), sem("ys_out")
        s_dve, s_act, s_pe = sem("s_dve"), sem("s_act"), sem("s_pe")
        mh_done, ml_done = sem("mh_done"), sem("ml_done")
        woh_done, wol_done = sem("woh_done"), sem("wol_done")
        y_done = sem("y_done")
        y_sq, y_rt, y_nrm, y_add = sem("y_sq"), sem("y_rt"), sem("y_nrm"), sem("y_add")
        dve_link, act_link, pool_link = sem("dve_link"), sem("act_link"), sem("pool_link")

        NCONST = 19
        X_ORDER = Y_ORDER = [NQ] + list(range(NQ))
        PAST = cck.shape[1]
        C_ROWS = [slice(PAST - 128, PAST), slice(PAST - 512, PAST, 4), slice(0, PAST, 16)]

        def bank_of(t, c):
            return (3 * t + c) % 5

        def kind(t):
            n = NAMES[t]
            return "gate" if n[0] == "g" else ("v" if n[0] == "v" else "kept")

        def gate_no(t, c):
            return 3 * sum(kind(i) == "gate" for i in range(t)) + c + 1

        def slot_of(name):
            return PASSING.index(name) % 3

        def passing_free(eng, name):
            i = PASSING.index(name)
            if i >= 3:
                before = PASSING[i - 3]
                if before[0] == "v":
                    eng.wait_ge(job, JOB_NO["turn", before, 1] + 1)
                else:
                    n = sum(slot_of(g) == slot_of(before) for g in GATES[:GATE_AT[before] + 1])
                    eng.wait_ge(gate_out[slot_of(before)], 16 * n)

        def dest(t):
            n = NAMES[t]
            return tile_of[n] if n in tile_of else passing[slot_of(n)]

        EARLY_MIX = 2
        FIRST = 2 * P

        def stacked(hh):
            return 16 * sum(4 if x < HA else 3 for x in range(hh % 2, hh + 1, 2))

        def stored(p):
            return 16 * sum(6 if x < 2 else 4 for x in range(p + 1))

        def keep_free(eng, it):
            i = ITEM_NO[it]
            if i >= 2:
                b = ITEMS[i - 2]
                if b[0] == "s":
                    eng.wait_ge(score_read, SCORE_NO[b] + 1)
                else:
                    eng.wait_ge(item_read, OTHER_NO[b] + 1)

        def score_bank(it):
            return flat[:, (ITEM_NO[it] % 2) * S:(ITEM_NO[it] % 2 + 1) * S]

        ALL_CHUNKS = 3 * NT
        NGATE = 3 * len(GATES)

        def stage1_over(eng):
            eng.wait_ge(proj, ALL_CHUNKS)
            eng.wait_ge(evac, ALL_CHUNKS)
            eng.wait_ge(gated, NGATE)
            eng.wait_ge(job_out, len(JOBS))

        def gates_stored(eng):
            for i in range(3):
                eng.wait_ge(gate_out[i], 16 * sum(slot_of(g) == i for g in GATES))

        def a_tail(eng):
            eng.wait_ge(res_done, NB)
            eng.wait_ge(res_c_done, NB)

        def y_before(i):
            return ys_raw[:] if i == 0 else flat[:, ((i - 1) % 3) * D:((i - 1) % 3 + 1) * D]

        block = ctx.enter_context(nc.Block())

        @block.sync
        def _(sp):
            n_const = [0]

            def load(dst, src, slow=False):
                sp.dma_start(dst, src, allow_slow_non_contiguous=slow).then_inc(consts_in, 16)
                n_const[0] += 1

            def load_x(i):
                if i >= 3:
                    sp.wait_ge(xn_done, i - 2)
                s = X_ORDER[i]
                src = x_d[s * P:(s + 1) * P, :] if s < NQ else xs_d
                n = P if s < NQ else NB
                sp.dma_start(xraw[i % 3][0:n, :], src).then_inc(x_in[i % 3], 16)

            def load_w(t):
                if t >= 3:
                    sp.wait_ge(wl_done, t - 2)
                c = TILES[t][1]
                sp.dma_start(wraw[t % 3][:], w_in[:, :, c:c + P]).then_inc(w_landed[t % 3], 16)

            pt = a["page_table"].rearrange("b j -> j b")
            load_x(0)
            sp.dma_start(ident[:], a["c_ident"]).then_inc(first_in, 16)
            sp.dma_start(g_pre[:], a["ln_pre"][0].partition_broadcast(P)).then_inc(first_in, 16)
            load_x(1)
            load_w(0)
            load_x(2)
            load_w(1)
            for q in range(QPP):
                sp.dma_start(pageT[q:q + QPP * (PAGES - 1) + 1:QPP, :], pt, allow_slow_non_contiguous=True)\
                  .then_inc(pages_in, 16)
            sp.dma_start(quarter[:], a["c_quarter"]).then_inc(pages_in, 16)
            for i in range(3, NQ + 1):
                load_x(i)
            sp.wait_ge(early_out, 2)
            sp.dma_start(q_d[0], rows[1][:, 0:W_BR]).then_inc(q_out, 16)
            sp.wait_ge(q_out, 16)
            for b in range(2):
                sp.dma_start(qrep[b][:], q_d[0, b].partition_broadcast(P)).then_inc(q_in[b], 16)
            load_w(2)
            load(bones[:], a["c_bones"])
            load(sel[:], a["c_sel"])
            load(prow[0:4, :], a["conv_w"][0])
            load(prow[4:5, :], a["conv_b"])
            load(prow[5:6, :], a["b_rgate"])
            load(prow[6:7, :], a["b_igate"])
            load(prow[7:8, :], a["lru_lambda"])
            load(srow[0:24, :], a["state_conv"].rearrange("l b k d -> (l b k) d"))
            load(srow[24:32, :], a["state_lru"][0])
            for i, n in enumerate(("lam_q1", "lam_q2", "lam_k1", "lam_k2")):
                load(lamv[:, i, :], a[n][0].partition_broadcast(P))
            for r in range(2):
                load(gsub[64 * r:64 * r + 64, :], a["subln_g"].rearrange("l d -> d l"), slow=True)
            sp.wait_ge(setup_done, 1)
            for g, n in enumerate(("w_rgate", "w_igate")):
                w = a[n][0].rearrange("(f r) d e -> r d f e", r=2)
                for r in range(2):
                    load(bdiag[64 * r:64 * r + 64, :, g, 64 * r:64 * r + 64], w[r])
            assert n_const[0] == NCONST, n_const
            cs = cn_s[0]
            sp.dma_start(cs[:, 0:2, :], a["state_conv"][0][:, 1:3, :]).then_inc(misc_out, 16)

            def store_pair(p, e):
                for g in range(2):
                    src = ((QH, QL), (KH, KL))[e][g]
                    sp.wait_ge(split_done, 4 * p + 2 * e + g + 1)
                    if p >= 2:
                        dst = kc_d[p - 2, g] if e else qc_d[p - 2, :, g]
                        sp.dma_start(dst, src[:].bitcast(F32)).then_inc(qk_out, 16)
                    else:
                        for i in ((2 * g, 2 * g + 1) if e else (g,)):
                            dst = (ka_d if e else qa_d)[p, :, i]
                            sp.dma_start(dst, src[:].bitcast(F32)).then_inc(qk_out, 16)

            turn_no = [0]
            for step in range(PSTEPS + 8):
                t, kt = divmod(step, KT)
                if kt == 0 and 1 <= t and t + 2 < NT:
                    load_w(t + 2)
                if step - 10 in SPLIT_AT and SPLIT_AT.index(step - 10) % 2:
                    store_pair(0, SPLIT_AT.index(step - 10) // 2)
                ji = JOB_AT.get(step - 1)
                if ji is not None:
                    _, k, arg, h = JOBS[ji]
                    if k == "turn" and h == 1:
                        sp.wait_ge(job_out, ji + 1)
                        i = turn_no[0] % 2
                        f = int(arg[2]) * P
                        sp.dma_start(nat_out[arg[:2]][:, :, f:f + P], nat[i][:]).then_inc(nat_out_done[i], 16)
                        turn_no[0] += 1
                    if k == "rows":
                        sp.wait_ge(job_out, ji + 1)
                        r = rows[arg % 2]
                        n = (("qa", "ka"), ("va", "vc"), ("qc", "kc"), None)[arg]
                        if n is None:
                            sp.dma_start(cs[:, 2, :], r[:]).then_inc(rows_out[1], 16)
                        else:
                            for i, m in enumerate(n):
                                if m == "qa":
                                    continue
                                dst = q_d[1] if m == "qc" else row_out[m]
                                sp.dma_start(dst, r[:, i * W_BR:(i + 1) * W_BR]).then_inc(rows_out[arg % 2], 16)
                        if arg in (0, 2):
                            e = arg // 2
                            w = (HCA, HC)[e]
                            sp.wait_ge(snat_done, e + 1)
                            sp.dma_start(sn_d[e, :, 0:w], snat[:, 8 * e:8 * e + w]).then_inc(snat_out, 16)
                            sp.wait_ge(snat_out, 16 * (e + 1))
                            sp.wait_ge(rows_out[0], (16, 48)[e])
                            dst = (sn_a, sn_c)[e]
                            sp.dma_start(dst[:], sn_d[e, :, 0:w].partition_broadcast(P)).then_inc(sn_in[e], 16)
                    if k == "tail":
                        sp.wait_ge(job_out, ji + 1)
                        sp.dma_start(cn_p[0, 0], tail).then_inc(tail_out, 16)
                n = K_AT.get(step - 1)
                if n is not None and n % NCH == NCH - 1 and 2 <= n // NCH + 2 < NB:
                    b = n // NCH + 2
                    sp.wait_ge(k_used, n + 1)
                    sp.dma_start(qrep[b % 2][:], q_d[0, b].partition_broadcast(P)).then_inc(q_in[b % 2], 16)
                b = C_STEP.get(step + 5)
                if b is not None:
                    if b >= 1:
                        sp.wait_ge(kc_used, b)
                    sp.dma_start(qrep_c[:], q_d[1, b].partition_broadcast(P)).then_inc(qc_in, 16)
                    for i, r in enumerate(C_ROWS):
                        sp.dma_start(kc[:, i, :], cck[b, r, :]).then_inc(kc_in, 16)
                    if b >= 2:
                        sp.wait_ge(job, JOB_NO["cpv", b - 2, 0] + 1)
                    for i, r in enumerate(C_ROWS):
                        sp.dma_start(vc[b % 2][:, i, :], ccv[b, r, :]).then_inc(vc_in[b % 2], 16)
                if kt == 1 and t >= 1 and t - 1 < NT and kind(t - 1) == "gate":
                    sp.wait_ge(gated, gate_no(t - 1, 2))
                    i = slot_of(NAMES[t - 1])
                    sp.dma_start(gate_d[GATE_AT[NAMES[t - 1]]], passing[i][:]).then_inc(gate_out[i], 16)

            sp.wait_ge(proj, ALL_CHUNKS)

            def load_stack(hh, c0=0, c1=S, arrived=None):
                sl = stack[hh % 2]
                arrived = arrived or stack_in[hh % 2]
                p = hh // 2
                sp.wait_ge(qk_out, stored(p))
                if hh >= 2:
                    last = UNITS.index((hh - 2, NQ - 1))
                    sp.wait_ge(scored, ITEM_NO["s", last, 1 if hh - 2 < HA else 0] + 1)
                if hh < HA:
                    for c in range(2):
                        i = 2 * (hh % 2) + c
                        q = qa_d[p, i].rearrange("g r n -> (g r) n")[:, c0:c1].unsqueeze(0).to_broadcast([2, 2 * DKA, c1 - c0])
                        k = ka_d[p, i].rearrange("g r n -> (g r) n")[:, c0:c1]
                        sp.dma_start(sl[2 * c][:, c0:c1].bitcast(F32), q).then_inc(arrived, 16)
                        sp.dma_start(sl[2 * c + 1][:, c0:c1].bitcast(F32), k).then_inc(arrived, 16)
                else:
                    r = DHC * (hh % 2)
                    sp.dma_start(sl[0][:].bitcast(F32), qc_d[p - 2, hh % 2].rearrange("g r n -> (g r) n")).then_inc(arrived, 16)
                    for g in range(2):
                        k = kc_d[p - 2, g, r:r + DHC, :].unsqueeze(0).to_broadcast([2, DHC, S])
                        sp.dma_start(sl[1 + g][:].bitcast(F32), k).then_inc(arrived, 16)

            def load_wo(k):
                if k < 2:
                    sp.wait_ge(split_done, 16)
                else:
                    sp.wait_ge(wol_done, k - 1)
                sp.dma_start(wo_raw[k % 2], w_out[k]).then_inc(wo_in[k % 2], 16)

            load_stack(0, 0, FIRST, first_stack)
            sp.dma_start(mask_a[:], a["c_mask_a"]).then_inc(mask_in, 16)
            load_stack(0, FIRST, S)
            gates_stored(sp)
            sp.dma_start(v_a[:], nat_out["va"]).then_inc(va_in, 16)
            load_stack(1)
            sp.dma_start(mask_c[:], a["c_mask_c"]).then_inc(late_in, 16)
            for u in range(NU + 1):
                h, q = UNITS[u] if u < NU else (8, 0)
                if q == NQ - 1 and h in (0, 2, 4):
                    store_pair(h // 2 + 1, 0)
                    store_pair(h // 2 + 1, 1)
                if q == 1 and h >= 1 and h + 1 < 8:
                    load_stack(h + 1)
                if u == UNITS.index((HA, 2)):
                    sp.wait_ge(scored, ITEM_NO["s", UNITS.index((HA, 1)), 0] + 1)
                    sp.wait_ge(split_done, 8)
                    sp.dma_start(v_c[:], nat_out["vc"]).then_inc(vc_nat_in, 16)
                if u == min(WO_AT) - 1:
                    load_wo(0)
                    load_wo(1)
                if u - 1 in WO_AT and WO_AT[u - 1] + 2 < KT:
                    load_wo(WO_AT[u - 1] + 2)
                if u - 11 in LRU_AT:
                    f = LRU_AT[u - 11]
                    sp.wait_ge(lru_in, f + 1)
                    sp.dma_start(TMP[1][:], gate_d[GATE_AT[f"gb{f}"]]).then_inc(gate_in, 16)
                    sp.wait_ge(lru_last, f + 1)
                    sp.dma_start(lr_p[0, 0, f * P:(f + 1) * P].unsqueeze(1), w1[:, 10, f:f + 1],
                                 allow_slow_non_contiguous=True).then_inc(misc_out, 16)
                if u in NORM_AT:
                    p = NORM_AT[u]
                    if p == 0:
                        sp.wait_ge(lru_h, 4)
                    else:
                        sp.wait_ge(nrm_done, 1)
                    sp.dma_start(TMP[2][:], gate_d[GATE_AT[f"ga{p}"]]).then_inc(norm_gate_in, 16)
                if u == MIX_C_AT - 4:
                    sp.wait_ge(lru_h, 4)
                    sp.dma_start(TMP[3][:], gate_d[GATE_AT["gc0"]]).then_inc(c_gate_in[0], 16)
                if u - 4 in NORM_AT and NORM_AT[u - 4] == 1:
                    sp.wait_ge(scored, ITEM_NO["norm", 1, 0] + 1)
                    sp.dma_start(TMP[0][:], gate_d[GATE_AT["gc1"]]).then_inc(c_gate_in[1], 16)
            sp.wait_ge(mix_c, 1)
            sp.dma_start(g_post[:], a["ln_post"][0].partition_broadcast(P)).then_inc(gpost_in, 16)
            for f in range(4):
                sp.dma_start(lr_s[0].rearrange("b (f p) -> f p b", p=P)[f], w1[:, 11, NB * f:NB * (f + 1)],
                             allow_slow_non_contiguous=True).then_inc(misc_out, 16)
            sp.wait_ge(ml_done, 6)

            def load_res(i):
                if i >= 2:
                    sp.wait_ge(y_add, i - 1)
                s = Y_ORDER[i]
                src = x_d[s * P:(s + 1) * P, :] if s < NQ else xs_d
                sp.dma_start(x_res[i % 2][0:P if s < NQ else NB, :], src).then_inc(res_in[i % 2], 16)

            load_res(0)
            load_res(1)
            for i, s in enumerate(Y_ORDER):
                sp.wait_ge(y_add, i + 1)
                n = P if s < NQ else NB
                dst = y_p[s * P:(s + 1) * P, :] if s < NQ else y_s
                sp.dma_start(dst, y_sb[i % 2][0:n, :]).then_inc(y_out[i % 2], 16)
                if i + 2 <= NQ:
                    load_res(i + 2)
            sp.wait_ge(y_out[0], 16 * 5)
            sp.wait_ge(y_out[1], 16 * 4)
            sp.wait_ge(misc_out, 16 * 9)
            sp.wait_ge(tail_out, 16)
            sp.wait_ge(rows_out[0], 48)
            sp.wait_ge(rows_out[1], 48)

        @block.gpsimd
        def _(pool):
            n_link = [0]

            def link(ins):
                n_link[0] += 1
                ins.then_inc(pool_link, 1)
                pool.wait_ge(pool_link, n_link[0])

            def split_w(t):
                pool.wait_ge(wh_done, t + 1)
                if t >= 2:
                    pool.wait_ge(proj, 3 * (t - 1))
                pool.tensor_tensor(wl[t % 2][:], wraw[t % 3][:], wh[t % 2][:].bitcast(F32), ALU.subtract)\
                    .then_inc(wl_done, 1)

            def load_k(n):
                if n >= 2:
                    pool.wait_ge(k_used, n - 1)
                b, c = divmod(n, NCH)
                pool.indirect_dma_start(kbuf[n % 2][:].rearrange("p s d -> p (s d)"), None, ck,
                                        bass.IndirectOffsetOnAxis(ap=index[:, b:b + 1], axis=0),
                                        element_offset=c * CH * W_BR).then_inc(k_in[n % 2], 16)

            def load_v(m):
                if m >= 3:
                    pool.wait_ge(v_used, m - 2)
                b, c = divmod(m, NCH)
                pool.indirect_dma_start(vbuf[m % 3][:].rearrange("p s d -> p (s d)"), None, cv,
                                        bass.IndirectOffsetOnAxis(ap=index[:, b:b + 1], axis=0),
                                        element_offset=c * CH * W_BR).then_inc(v_in[m % 3], 16)

            def sample_events(step):
                n = K_AT.get(step - 1)
                if n is not None:
                    if n + 2 < NK:
                        load_k(n + 2)
                if step - 1 in MAX_AT:
                    b = MAX_AT[step - 1]
                    pool.wait_ge(mx_done, b + 1)
                    pool.partition_all_reduce(m_a[:, b, :], mx_a[:, b, :], P, RMAX).then_inc(m_done, 1)
                m = V_AT.get(step - 1)
                if m is not None and m + 3 < NK:
                    load_v(m + 3)
                b = C_STEP.get(step - 1)
                if b is not None:
                    pool.wait_ge(mxc_done, b + 1)
                    pool.partition_all_reduce(m_c[:, b, :], mx_c[:, b, :], P, RMAX).then_inc(mc_done, 1)

            split_w(0)
            split_w(1)
            pool.wait_ge(index_done, 1)
            for n in range(2):
                load_k(n)
            for m in range(3):
                load_v(m)

            def split_pair(p, i):
                if p == 0 and i == 0:
                    for j in range(2):
                        pool.wait_ge(nat_out_done[j], 16 * 4)
                    pool.wait_ge(evac, 3 * (TI["ka0"] + 1))
                if p == 0 and i == 2:
                    pool.wait_ge(kc_used, NB)
                    pool.wait_ge(job, JOB_NO["cpv", NB - 1, 0] + 1)
                if p >= 1 and i == 0:
                    pool.wait_ge(qk_out, stored(p - 1))
                src = tile_of[(("qa0", "qa1", "qc0", "qc1"), ("ka0", "ka1", "kc0", "kc1"))[i // 2][p]][:, 0:S]
                high, low = ((QH, QL), (KH, KL))[i // 2]
                if i % 2 == 0:
                    pool.tensor_copy(high[:], src).then_inc(split_done, 1)
                else:
                    pool.wait_ge(split_done, 4 * p + i)
                    pool.tensor_tensor(low[:], src, high[:].bitcast(F32), ALU.subtract).then_inc(split_done, 1)

            for step in range(PSTEPS):
                t, kt = divmod(step, KT)
                if kt == 0 and 1 <= t and t + 1 < NT:
                    split_w(t + 1)
                sample_events(step)
                if step in SPLIT_AT:
                    split_pair(0, SPLIT_AT.index(step))

            for u in range(NU):
                h, q = UNITS[u]
                if 4 <= q and h in (0, 2, 4):
                    split_pair(h // 2 + 1, q - 4)
                sample_events(PSTEPS + 2 * u)
                sample_events(PSTEPS + 2 * u + 1)
                if u - 5 in LRU_AT:
                    f = LRU_AT[u - 5]
                    pool.wait_ge(lru_a, 2 * f + 1)
                    pool.tensor_tensor(tile_of[f"xb{f}"][:, 0:S], TMP[3][:, 0:S], TMP[3][:, 0:S], ALU.mult)\
                        .then_inc(lru_sq, 1)
                if u - 9 in LRU_AT:
                    f = LRU_AT[u - 9]
                    pool.wait_ge(lru_rt, f + 1)
                    pool.wait_ge(lru_xi, f + 1)
                    pool.tensor_tensor(TMP[2][:, 0:S], TMP[2][:, 0:S], TMP[1][:, 0:S], ALU.mult).then_inc(lru_in, 1)
                if u - 12 in LRU_AT:
                    f = LRU_AT[u - 12]
                    h = tile_of[f"xb{f}"]
                    pool.wait_ge(lru_last, f + 1)
                    pool.wait_ge(gate_in, 16 * (f + 1))
                    pool.tensor_tensor(h[:, 0:S], h[:, 0:S], TMP[1][:, 0:S], ALU.mult).then_inc(lru_mix, 1)
                if u in NORM_AT:
                    p = NORM_AT[u]
                    t = tile_of[f"qa{p}"]
                    pool.wait_ge(core_out, 2 * NQ * (p + 1))
                    pool.wait_ge(lru_mix, 4)
                    if p:
                        pool.wait_ge(nrm_done, 1)
                    pool.tensor_tensor(TMP[0][:, 0:S], t[:, 0:S], t[:, 0:S], ALU.mult).then_inc(sq_done, 1)
                if u in WO_AT:
                    k = WO_AT[u]
                    pool.wait_ge(woh_done, k + 1)
                    pool.tensor_tensor(wo[k][:, 1, :], wo_raw[k % 2], wo[k][:, 0, :].bitcast(F32), ALU.subtract)\
                        .then_inc(wol_done, 1)
                if u == MIX_C_AT:
                    t = tile_of["qc0"]
                    pool.wait_ge(core_out, 6 * NQ)
                    pool.wait_ge(c_gate_in[0], 16)
                    pool.tensor_tensor(t[:, 0:S], t[:, 0:S], TMP[3][:, 0:S], ALU.mult).then_inc(mix_c, 1)

        @block.scalar
        def _(act):
            n_link = [0]

            def link(ins):
                n_link[0] += 1
                ins.then_inc(act_link, 1)
                act.wait_ge(act_link, n_link[0])

            def split_w(t):
                act.wait_ge(w_landed[t % 3], 16 * (t // 3 + 1))
                if t >= 2:
                    act.wait_ge(proj, 3 * (t - 1))
                act.activation(wh[t % 2][:], wraw[t % 3][:], ACT.Copy).then_inc(wh_done, 1)

            def x_high(i):
                s = X_ORDER[i]
                w = P if s < NQ else NB
                for h in range(2):
                    u = 2 * i + h
                    act.wait_ge(x_turned, u + 1)
                    src = ps[:, u % 5, 0:4 * w].rearrange("p (k n) -> p k n", n=w)
                    act.activation(xh[:, 4 * h:4 * h + 4, s * P:s * P + w], src, ACT.Copy).then_inc(xh_done, 1)

            act.wait_ge(setup_done, 1)
            for i, s in enumerate(X_ORDER):
                n = P if s < NQ else NB
                act.wait_ge(x_in[i % 3], 16 * (i // 3 + 1))
                if i >= 2:
                    act.wait_ge(x_turned, 2 * (i - 1))
                act.activation(xn[i % 2][0:n, :], xraw[i % 3][0:n, :], ACT.Square, accum_out=ss[0:n, i:i + 1])\
                    .then_inc(squares, 1)
                act.wait_ge(squares, i + 1)
                act.activation(rstd[0:n, i:i + 1], ss[0:n, i:i + 1], ACT.Sqrt, bias=eps[0:n, 0:1], scale=1.0 / D)\
                    .then_inc(roots, 1)
                if i in (1, 2):
                    split_w(i - 1)
                if i >= 1:
                    x_high(i - 1)
                if i == 5:
                    act.wait_ge(early, 2)
                    act.activation(us[:, 0:2, :], ps[:, JB, 0:16].rearrange("p (t b) -> p t b", b=NB), ACT.Copy)\
                       .then_inc(early_out, 1)
                if i == 6:
                    act.wait_ge(early, 3)
                    act.activation(rows[1][:, 0:W_BR], ps[0:NB, JB, 0:W_BR], ACT.Copy).then_inc(early_out, 1)
            x_high(NQ)

            def evacuate(t):
                d, k = dest(t), kind(t)
                if k != "kept":
                    passing_free(act, NAMES[t])
                if t in (TI["xb0"], TI["xb1"], TI["xb2"], TI["xb3"]) or (t < 2):
                    act.wait_ge(xl_done, 18)
                for c in range(3):
                    act.wait_ge(proj, 3 * t + c + 1)
                    src = ps[:, bank_of(t, c), 0:CW]
                    ins = act.activation(d[:, c * CW:(c + 1) * CW], src, ACT.Tanh if k == "gate" else ACT.Copy,
                                         scale=0.5 if k == "gate" else 1.0)
                    if c == 2 and k != "gate" and t >= 2:
                        ins = act.activation(us[:, t, :], src[:, CW - NB:CW], ACT.Copy)
                    ins.then_inc(evac, 1)

            turn_no = [0]

            def job_evac(ji):
                _, k, arg, h = JOBS[ji]
                act.wait_ge(job, ji + 1)
                if k == "param":
                    ins = act.activation(pT[:], ps[:, JB, 0:32].rearrange("p (f n) -> p f n", n=8), ACT.Copy)
                elif k == "state":
                    ins = act.activation(sT[:], ps[:, JB, 0:128].rearrange("p (f n) -> p f n", n=32), ACT.Copy)
                elif k == "rows":
                    if arg >= 2:
                        act.wait_ge(rows_out[arg % 2], (16, 32)[arg % 2])
                        if arg == 2:
                            act.wait_ge(snat_done, 1)
                    if arg == 1:
                        act.wait_ge(q_out, 16)
                    ins = act.activation(rows[arg % 2][:], ps[0:NB, JB, :], ACT.Copy)
                elif k == "tail":
                    act.wait_ge(rows_out[0], 48)
                    act.wait_ge(snat_done, 2)
                    ins = act.activation(tail, ps[0:3, JB, :], ACT.Copy)
                elif k == "turn":
                    i = turn_no[0] // 2
                    if i >= 2:
                        act.wait_ge(nat_out_done[i % 2], 16 * (i // 2))
                    ins = act.activation(nat[i % 2][:, 4 * h:4 * h + 4, :],
                                         ps[:, JB, :].rearrange("p (k n) -> p k n", n=P), ACT.Copy)
                    turn_no[0] += 1
                elif k == "cpv":
                    act.wait_ge(acc_zero, 2)
                    if arg >= 1:
                        act.wait_ge(picked_c, arg)
                    for i in range(3):
                        ins = act.activation(acc_c[32 * i:32 * i + HC, :], ps[32 * i:32 * i + HC, JB, 0:W_BR], ACT.Copy)
                ins.then_inc(job_out, 1)

            def sample_events(step):
                if step - 2 in MAX_AT:
                    exp_a(MAX_AT[step - 2])
                m = V_AT.get(step - 1)
                if m is not None and m % NCH == NCH - 1:
                    b = m // NCH
                    act.wait_ge(v_used, m + 1)
                    act.wait_ge(acc_zero, 2)
                    if b >= 1:
                        act.wait_ge(picked, b)
                    for i in range(4):
                        ins = act.activation(acc[32 * i:32 * i + HCA, :],
                                             ps[32 * i:32 * i + HCA, VB, 0:W_BR], ACT.Copy)
                    ins.then_inc(acc_out, 1)
                if step in PICK_AT:
                    b = PICK_AT[step]
                    act.wait_ge(picked, b + 1)
                    act.activation(res_a[:, b, :], ps[:, RB, 0:24], ACT.Copy).then_inc(res_done, 1)
                b = C_STEP.get(step - 3)
                if b is not None:
                    act.wait_ge(subc_done, b + 1)
                    if b >= 2:
                        act.wait_ge(job, JOB_NO["cpv", b - 2, 0] + 1)
                        act.wait_ge(dsc_done, b - 1)
                    act.activation(ex_c[b % 2][:], sc_c[b % 2][:], ACT.Exp, scale=SCALE_C).then_inc(exc_done, 1)
                b = C_STEP.get(step - 8)
                if b is not None:
                    act.wait_ge(picked_c, b + 1)
                    act.activation(res_c[:, b, :], ps[:, RB, 32:44], ACT.Copy).then_inc(res_c_done, 1)

            def exp_a(b):
                act.wait_ge(sub_done, b + 1)
                if b >= 2:
                    act.wait_ge(v_used, NCH * (b - 1))
                    act.wait_ge(ds_done, b - 1)
                act.activation(ex[b % 2][:], sc[b % 2][:], ACT.Exp, scale=SCALE_A).then_inc(ex_done, 1)

            for step in range(PSTEPS + 8):
                t, kt = divmod(step, KT)
                if kt == 0:
                    if t >= 1:
                        evacuate(t - 1)
                    if 1 <= t and t + 1 < NT:
                        split_w(t + 1)
                    if t == 1:
                        act.wait_ge(s_dve, 1)
                        act.activation(lam2[:], lam2[:], ACT.Exp).then_inc(s_act, 1)
                    if t == 2:
                        act.wait_ge(s_dve, 3)
                        link(act.activation(sp[:, 0, :], pT[:, :, 7], ACT.Abs))
                        act.activation(sp[:, 1, :], sp[:, 0, :], ACT.Exp, scale=-1.0).then_inc(s_act, 1)
                        act.wait_ge(s_dve, 4)
                        act.activation(sp[:, 3, :], sp[:, 2, :], ACT.Ln).then_inc(s_act, 1)
                if step < PSTEPS:
                    sample_events(step)
                ji = JOB_AT.get(step)
                if ji is not None:
                    job_evac(ji)

            def exps(u):
                h, q = UNITS[u]
                w = (q + 1) * P
                for c in range(2 if h < HA else 1):
                    k = SCORE_NO["s", u, c]
                    e = (2 * u + c) % 4
                    act.wait_ge(score_read, k + 1)
                    if u >= 2:
                        act.wait_ge(pd_done, u - 1)
                        act.wait_ge(turned, GROUP_NO[u - 2, 1 if UNITS[u - 2][1] >= 4 else 0] + 1)
                    act.activation(E[e][:, 0:w], T[k % 2][:, 0:w], ACT.Exp, bias=negmax[:, k % 4:k % 4 + 1], scale=-1.0,
                                   accum_out=den[:, u % 4, c:c + 1]).then_inc(exped, 1)

            def pt_evac(u):
                h, q = UNITS[u]
                for g in range(2 if q >= 4 else 1):
                    nb = min(4, q + 1 - 4 * g)
                    i = GROUP_NO[u, g]
                    act.wait_ge(turned, i + 1)
                    if u >= 2:
                        act.wait_ge(attended, u - 1)
                    act.activation(PT[u % 2][:, 4 * g:4 * g + nb, :],
                                   ps[:, 4 + i % 2, 0:nb * P].rearrange("p (k n) -> p k n", n=P), ACT.Copy)\
                       .then_inc(pt_out, 1)

            def core_evac(u):
                h, q = UNITS[u]
                r = 64 * (h % 2)
                act.wait_ge(attended, u + 1)
                d = tile_of[("qa0", "qa1", "qc0", "qc1")[h // 2]]
                act.wait_ge(split_done, 4 * (h // 2 + 1))
                act.activation(d[r:r + 64, q * P:(q + 1) * P], ps[r:r + 64, RB, 128:256],
                               ACT.Copy).then_inc(core_out, 1)

            def other_items(u):
                for i in range(4):
                    if u - 2 - i in LRU_AT:
                        f, w, k0 = LRU_AT[u - 2 - i], i // 2, (i % 2) * 512
                        it = ("gate", f, i)
                        act.wait_ge(scored, ITEM_NO[it] + 1)
                        if i == 0 and f >= 1:
                            act.wait_ge(lru_mix, f)
                        act.activation(TMP[1 + w][:, k0:k0 + 512], score_bank(it)[:, 0:512], ACT.Tanh,
                                       bias=hb[:, f, w:w + 1], scale=0.5).then_inc(item_read, 1)
                if u - 4 in LRU_AT:
                    f = LRU_AT[u - 4]
                    act.wait_ge(item_read, OTHER_NO["gate", f, 1] + 1)
                    act.activation(TMP[3][:, 0:S], TMP[1][:, 0:S], ACT.Exp, bias=c4[:, f:f + 1], scale=c4[:, f:f + 1])\
                       .then_inc(lru_a, 1)
                if u - 6 in LRU_AT:
                    f = LRU_AT[u - 6]
                    act.wait_ge(lru_a, 2 * f + 1)
                    act.activation(TMP[1][:, 0:S], TMP[1][:, 0:S], ACT.Tanh, bias=nc4[:, f:f + 1], scale=nc4[:, f:f + 1])\
                       .then_inc(lru_a, 1)

            def root_steps(u):
                if u - 8 in LRU_AT:
                    act.wait_ge(lru_om, LRU_AT[u - 8] + 1)
                    act.activation(TMP[1][:, 0:S], TMP[1][:, 0:S], ACT.Sqrt).then_inc(lru_rt, 1)
                if u - 3 in NORM_AT:
                    p = NORM_AT[u - 3]
                    act.wait_ge(scored, ITEM_NO["norm", p, 0] + 1)
                    act.activation(TMP[1][:, 0:S], score_bank(("norm", p, 0)), ACT.Sqrt, bias=eps[:, 0:1])\
                       .then_inc(item_read, 1)

            def sample_last(i):
                if i == 1:
                    act.wait_ge(s_dve, 5)
                    act.activation(w1[:, 0, :].rearrange("p (b h) -> p b h", h=HC), m_c[:], ACT.Exp, scale=SCALE_C)
                    act.activation(ds_a[:], m_a[:], ACT.Exp, scale=SCALE_A).then_inc(s_act, 1)
                if i == 3:
                    act.wait_ge(s_dve, 6)
                    act.activation(w1[:, 2:4, :], w1[:, 2:4, :], ACT.Tanh, scale=0.5).then_inc(s_act, 1)
                if i == 5:
                    act.wait_ge(s_dve, 7)
                    act.activation(w1[:, 4, :], w1[:, 2, :], ACT.Exp)
                    act.activation(w1[:, 5, :], w1[:, 2, :], ACT.Tanh, scale=-1.0).then_inc(s_act, 1)
                if i == 7:
                    act.wait_ge(s_dve, 8)
                    act.activation(w1[:, 5, :], w1[:, 5, :], ACT.Sqrt).then_inc(s_act, 1)
                if i == 11:
                    act.wait_ge(s_pe, 2)
                    act.activation(w1[:, 9, 0:16], ps[:, VB, 64:80], ACT.Sqrt, bias=eps[:, 0:1]).then_inc(s_act, 1)
                if i == 14:
                    act.wait_ge(smix, 1)
                    act.activation(sxh[:], w1[:, 6:8, :].rearrange("p a (k b) -> p (a k) b", b=NB), ACT.Copy)\
                       .then_inc(sxh_done, 1)

            def mix_high(k):
                n = MIX[k]
                if n[0] == "x":
                    act.wait_ge(lru_mix, k - 1)
                elif n[1] == "a":
                    act.wait_ge(nrm_done, k + 1)
                else:
                    act.wait_ge(mix_c, k - 5)
                act.activation(mh[:, k, NB:SW], tile_of[n][:, 0:S], ACT.Copy, scale=mix_scale(n)).then_inc(mh_done, 1)

            def split_wo(k):
                if k == 0:
                    gates_stored(act)
                    act.wait_ge(k_used, NK)
                    act.wait_ge(v_used, NK)
                    act.wait_ge(kc_used, NB)
                    act.wait_ge(ds_done, NB)
                    act.wait_ge(picked, NB)
                    act.wait_ge(picked_c, NB)
                    act.wait_ge(attended, HA * NQ)
                    act.wait_ge(qk_out, stored(3))
                act.wait_ge(wo_in[k % 2], 16 * (k // 2 + 1))
                act.activation(wo[k][:, 0, :], wo_raw[k % 2], ACT.Copy).then_inc(woh_done, 1)

            stage1_over(act)
            for u in range(NU + 2):
                if u < NU:
                    exps(u)
                if 0 <= u < NU:
                    root_steps(u)
                if u >= 2:
                    core_evac(u - 2)
                if 1 <= u <= NU:
                    pt_evac(u - 1)
                if u == NU:
                    act.wait_ge(scored, len(ITEMS))
                    for k in range(EARLY_MIX):
                        mix_high(k)
                if 0 <= u < NU:
                    other_items(u)
                    sample_last(u - SAMPLE_AT)
                    if u in WO_AT:
                        split_wo(WO_AT[u])
                    if YS_AT.get(u - 1) in (3, 7):
                        i = YS_AT[u - 1] // 4
                        act.wait_ge(ys_part, i + 1)
                        act.wait_ge(rows_out[i], 48)
                        act.wait_ge(tail_out, 16)
                        act.activation(ys_raw[:, i * 512:(i + 1) * 512], ps[0:NB, VB, :], ACT.Copy).then_inc(ys_out, 1)
                if u < NU:
                    sample_events(PSTEPS + 2 * u)
                    sample_events(PSTEPS + 2 * u + 1)
            act.wait_ge(attended, NU)
            a_tail(act)
            for k in range(EARLY_MIX, KT):
                mix_high(k)
            for s in range(NQ + 1):
                n = P if s else NB
                src = y_before(s)
                if s == 0:
                    act.wait_ge(ml_done, 6)
                    act.wait_ge(ys_out, 2)
                else:
                    act.wait_ge(y_done, s)
                if s >= 2:
                    act.wait_ge(y_out[s % 2], 16 * (s // 2))
                act.activation(y_sb[s % 2][0:n, :], src, ACT.Square, accum_out=yss[0:n, s:s + 1]).then_inc(y_sq, 1)
                act.wait_ge(y_sq, s + 1)
                act.activation(yrs[0:n, s:s + 1], yss[0:n, s:s + 1], ACT.Sqrt, bias=eps[0:n, 0:1], scale=1.0 / D)\
                   .then_inc(y_rt, 1)

        @block.vector
        def _(dve):
            n_link = [0]

            def link(ins):
                n_link[0] += 1
                ins.then_inc(dve_link, 1)
                dve.wait_ge(dve_link, n_link[0])

            dve.memset(eps[:], EPS)
            dve.memset(acc[:], 0.0)
            dve.memset(acc_c[:], 0.0).then_inc(acc_zero, 2)
            dve.memset(ones[:], 1.0)
            dve.memset(bdiag[:], 0.0).then_inc(setup_done, 1)

            def x_low(i):
                s = X_ORDER[i]
                w = P if s < NQ else NB
                for h in range(2):
                    u = 2 * i + h
                    dve.wait_ge(xh_done, u + 1)
                    src = ps[:, u % 5, 0:4 * w].rearrange("p (k n) -> p k n", n=w)
                    dve.tensor_tensor(xl[:, 4 * h:4 * h + 4, s * P:s * P + w], src,
                                      xh[:, 4 * h:4 * h + 4, s * P:s * P + w].bitcast(F32), ALU.subtract)\
                       .then_inc(xl_done, 1)

            dve.wait_ge(first_in, 32)
            for i, s in enumerate(X_ORDER):
                n = P if s < NQ else NB
                dve.wait_ge(roots, i + 1)
                link(dve.reciprocal(rstd[0:n, i:i + 1], rstd[0:n, i:i + 1]))
                dve.scalar_tensor_tensor(out=xn[i % 2][0:n, :], in0=xraw[i % 3][0:n, :], scalar=rstd[0:n, i:i + 1],
                                         in1=g_pre[0:n, :], op0=ALU.mult, op1=ALU.mult).then_inc(xn_done, 1)
                if i >= 1:
                    x_low(i - 1)
                if i == 2:
                    dve.wait_ge(pages_in, 16 * 5)
                    dve.tensor_scalar(index[:], pageT[:], float(QPP), quarter[:, 0:1], ALU.mult, ALU.add)\
                       .then_inc(index_done, 1)
            x_low(NQ)

            def gate_chunks(t):
                d = passing[slot_of(NAMES[t])]
                for c in range(3):
                    dve.wait_ge(evac, 3 * t + c + 1)
                    src = ps[:, bank_of(t, c), 0:CW]
                    part = d[:, c * CW:(c + 1) * CW]
                    if c == 2:
                        link(dve.scalar_tensor_tensor(out=us[:, t, :], in0=part[:, CW - NB:CW], scalar=1.0,
                                                      in1=src[:, CW - NB:CW], op0=ALU.add, op1=ALU.mult))
                    dve.scalar_tensor_tensor(out=part, in0=part, scalar=1.0, in1=src, op0=ALU.add, op1=ALU.mult)\
                       .then_inc(gated, 1)

            def new_scores(e):
                w, d = ((HCA, DKA), (HC, DHC))[e]
                dve.wait_ge(job_out, JOB_NO["rows", 2 * e, 0] + 1)
                r = rows[0]
                tmp = prod[0:NB, 0, :]
                if k_done[0]:
                    dve.wait_ge(k_used, k_done[0])
                link(dve.tensor_tensor(tmp, r[:, 0:W_BR], r[:, W_BR:2 * W_BR], ALU.mult))
                dve.tensor_reduce(snat[:, 8 * e:8 * e + w], tmp.rearrange("p (h d) -> p h d", d=d), AX, ALU.add)\
                   .then_inc(snat_done, 1)
                dve.wait_ge(snat_done, e + 1)

            k_done = [0]

            def k_chunk(n):
                b, c = divmod(n, NCH)
                dve.wait_ge(k_in[n % 2], 16 * (n // 2 + 1))
                if c == 0:
                    dve.wait_ge(q_in[b % 2], 16 * (b // 2 + 1))
                if n >= 1:
                    dve.wait_ge(k_used, n)
                if c == 0 and b >= 2:
                    dve.wait_ge(ex_done, b - 1)
                link(dve.tensor_tensor(prod[:], kbuf[n % 2][:], qrep[b % 2][:].unsqueeze(1).to_broadcast([P, CH, W_BR]),
                                       ALU.mult))
                dve.tensor_reduce(sc[b % 2][:, CH * c:CH * (c + 1), :],
                                  prod[:].rearrange("p s (h d) -> p s h d", d=DKA), AX, ALU.add).then_inc(k_used, 1)
                k_done[0] = n + 1

            def row_max(b):
                dve.wait_ge(sn_in[0], 16)
                dve.wait_ge(k_used, NCH * (b + 1))
                link(dve.tensor_reduce(mx_a[:, b, :], sc[b % 2][:].rearrange("p s h -> p h s"), AX, ALU.max))
                dve.tensor_tensor(mx_a[:, b, :], mx_a[:, b, :], sn_a[:, b, :], ALU.max).then_inc(mx_done, 1)

            def subtract_max(b):
                dve.wait_ge(m_done, b + 1)
                dve.tensor_tensor(sc[b % 2][:], sc[b % 2][:], m_a[:, b, :].unsqueeze(1).to_broadcast([P, PPP, HCA]),
                                  ALU.subtract).then_inc(sub_done, 1)

            def sum_exps(b):
                dve.wait_ge(ex_done, b + 1)
                dve.tensor_reduce(ds_a[:, b, :], ex[b % 2][:].rearrange("p s h -> p h s"), AX, ALU.add)\
                   .then_inc(ds_done, 1)

            def c_scores(b):
                dve.wait_ge(kc_in, 48 * (b + 1))
                dve.wait_ge(qc_in, 16 * (b + 1))
                if b == 0:
                    dve.wait_ge(sn_in[1], 16)
                if k_done[0]:
                    dve.wait_ge(k_used, k_done[0])
                if b >= 2:
                    dve.wait_ge(exc_done, b - 1)
                link(dve.tensor_tensor(prod[:, 0:3, :], kc[:], qrep_c[:].unsqueeze(1).to_broadcast([P, 3, W_BR]), ALU.mult))
                dve.tensor_reduce(sc_c[b % 2][:], prod[:, 0:3, :].rearrange("p s (h d) -> p s h d", d=DHC), AX, ALU.add)\
                   .then_inc(kc_used, 1)
                dve.wait_ge(kc_used, b + 1)
                link(dve.tensor_reduce(mx_c[:, b, :], sc_c[b % 2][:].rearrange("p s h -> p h s"), AX, ALU.max))
                dve.tensor_tensor(mx_c[:, b, :], mx_c[:, b, :], sn_c[:, b, :], ALU.max).then_inc(mxc_done, 1)

            def sample_events(step):
                n = K_AT.get(step)
                if n is not None:
                    k_chunk(n)
                b = C_STEP.get(step)
                if b is not None:
                    c_scores(b)
                if step in MAX_AT:
                    row_max(MAX_AT[step])
                if step - 2 in MAX_AT:
                    subtract_max(MAX_AT[step - 2])
                if step - 4 in MAX_AT:
                    sum_exps(MAX_AT[step - 4])
                b = C_STEP.get(step - 2)
                if b is not None:
                    dve.wait_ge(mc_done, b + 1)
                    dve.tensor_tensor(sc_c[b % 2][:], sc_c[b % 2][:], m_c[:, b, :].unsqueeze(1).to_broadcast([P, 3, HC]),
                                      ALU.subtract).then_inc(subc_done, 1)
                b = C_STEP.get(step - 4)
                if b is not None:
                    dve.wait_ge(exc_done, b + 1)
                    dve.tensor_reduce(ds_c[:, b, :], ex_c[b % 2][:].rearrange("p s h -> p h s"), AX, ALU.add)\
                       .then_inc(dsc_done, 1)

            for step in range(PSTEPS + 8):
                t, kt = divmod(step, KT)
                if kt == 0 and 1 <= t and kind(t - 1) == "gate":
                    gate_chunks(t - 1)
                if step < PSTEPS:
                    sample_events(step)
                ji = JOB_AT.get(step)
                if ji is not None and JOBS[ji][1] == "rows" and JOBS[ji][2] in (0, 2):
                    new_scores(JOBS[ji][2] // 2)
                if step == KT - 1:
                    dve.wait_ge(consts_in, 16 * NCONST)
                    link(dve.tensor_tensor(lamp[:], lamv[:, 0:2, :], lamv[:, 2:4, :], ALU.mult))
                    dve.tensor_reduce(lam2[:], lamp[:], AX, ALU.add).then_inc(s_dve, 1)
                if step == 2 * KT - 1:
                    dve.wait_ge(s_act, 1)
                    link(dve.tensor_tensor(neglam[:], lam2[:, 1:2], lam2[:, 0:1], ALU.subtract))
                    dve.tensor_scalar(neglam[:], neglam[:], LAM_INIT, None, ALU.subtract).then_inc(s_dve, 1)
                    dve.wait_ge(job_out, JOB_NO["param", 0, 0] + 1)
                    dve.tensor_scalar(hb[:], pT[:, :, 5:7], 0.5, None, ALU.mult).then_inc(s_dve, 1)
                    dve.wait_ge(s_act, 2)
                    e, w = sp[:, 1, :], sp[:, 2, :]
                    dve.tensor_scalar(w, e, 1.0, None, ALU.add).then_inc(s_dve, 1)
                    dve.wait_ge(s_act, 3)
                    link(dve.tensor_scalar(sp[:, 4, :], w, 1.0, None, ALU.is_equal))
                    link(dve.scalar_tensor_tensor(out=sp[:, 5, :], in0=w, scalar=-1.0, in1=sp[:, 4, :], op0=ALU.add,
                                                  op1=ALU.add))
                    link(dve.reciprocal(sp[:, 5, :], sp[:, 5, :]))
                    link(dve.tensor_tensor(sp[:, 4, :], sp[:, 3, :], sp[:, 4, :], ALU.add))
                    link(dve.tensor_tensor(sp[:, 4, :], sp[:, 4, :], sp[:, 5, :], ALU.mult))
                    link(dve.tensor_tensor(sp[:, 4, :], sp[:, 4, :], e, ALU.mult))
                    link(dve.tensor_scalar(sp[:, 5, :], pT[:, :, 7], -1.0, 0.0, ALU.mult, ALU.max))
                    link(dve.tensor_tensor(sp[:, 4, :], sp[:, 4, :], sp[:, 5, :], ALU.add))
                    dve.tensor_scalar(c4[:], sp[:, 4, :], -4.0, None, ALU.mult)
                    link(dve.tensor_scalar(nc4[:], sp[:, 4, :], 4.0, None, ALU.mult))

            stage1_over(dve)
            dve.wait_ge(mask_in, 16)

            def mask_scores(u):
                h, q = UNITS[u]
                w = (q + 1) * P
                scale, mask = (SCALE_A, mask_a) if h < HA else (SCALE_C, mask_c)
                if h == HA and q == 0:
                    dve.wait_ge(late_in, 16)
                for c in range(2 if h < HA else 1):
                    it = ("s", u, c)
                    k = SCORE_NO[it]
                    dve.wait_ge(scored, ITEM_NO[it] + 1)
                    if k >= 2:
                        dve.wait_ge(exped, k - 1)
                    dve.tensor_tensor_reduce(T[k % 2][:, 0:w], score_bank(it)[:, 0:w], mask[:, S - w:S], -scale, 3.0e38,
                                             ALU.add, ALU.min, negmax[:, k % 4:k % 4 + 1]).then_inc(score_read, 1)

            def probs(u):
                h, q = UNITS[u]
                w = (q + 1) * P
                n = 2 if h < HA else 1
                e0, e1 = E[2 * u % 4], E[(2 * u + 1) % 4]
                d, r = den[:, u % 4, 0:n], rden[:, u % 4, 0:n]
                dve.wait_ge(exped, SCORE_NO["s", u, n - 1] + 1)
                link(dve.reciprocal(r, d))
                if h < HA:
                    link(dve.tensor_scalar(e1[:, 0:w], e1[:, 0:w], rden[:, u % 4, 1:2], neglam[:, 0:1], ALU.mult, ALU.mult))
                    dve.scalar_tensor_tensor(out=e0[:, 0:w], in0=e0[:, 0:w], scalar=rden[:, u % 4, 0:1], in1=e1[:, 0:w],
                                             op0=ALU.mult, op1=ALU.add).then_inc(pd_done, 1)
                else:
                    dve.tensor_scalar(e0[:, 0:w], e0[:, 0:w], rden[:, u % 4, 0:1], None, ALU.mult).then_inc(pd_done, 1)

            def conv(f, part):
                x, y = tile_of[f"xb{f}"], TMP[0]
                if f == 0 and part == 0:
                    gates_stored(dve)
                if f >= 1 and part == 0:
                    dve.wait_ge(lru_xi, f)
                    dve.wait_ge(scored, ITEM_NO["gate", f - 1, 3] + 1)
                if part == 0:
                    link(dve.tensor_scalar(y[:, 0:S], x[:, 0:S], pT[:, f, 3:4], pT[:, f, 4:5], ALU.mult, ALU.add))
                    link(dve.scalar_tensor_tensor(out=y[:, 1:S], in0=x[:, 0:S - 1], scalar=pT[:, f, 2:3],
                                                  in1=y[:, 1:S], op0=ALU.mult, op1=ALU.add))
                else:
                    link(dve.scalar_tensor_tensor(out=y[:, 2:S], in0=x[:, 0:S - 2], scalar=pT[:, f, 1:2],
                                                  in1=y[:, 2:S], op0=ALU.mult, op1=ALU.add))
                    dve.scalar_tensor_tensor(out=y[:, 3:S], in0=x[:, 0:S - 3], scalar=pT[:, f, 0:1], in1=y[:, 3:S],
                                             op0=ALU.mult, op1=ALU.add).then_inc(conv_done, 1)

            r3 = lambda i, n, m: w1[:, i, 0:n * m].rearrange("p (a b) -> p a b", b=m)
            sx = us[:, TI["xb0"]:TI["xb0"] + 4, :]
            st = sT[:, :, 0:24].rearrange("p f (b k) -> p f b k", k=3)
            h0 = sT[:, :, 24:32]
            mix = w1[:, 6:8, :].rearrange("p a (k b) -> p (a k) b", b=NB)
            oa = r3(3, 2, NB)

            def par(i):
                return pT[:, :, i:i + 1].to_broadcast([P, 4, NB])

            def sample_last(i):
                if i == 0:
                    a_tail(dve)
                    dve.tensor_tensor(m_c[:], sn_c[:], m_c[:], ALU.subtract)
                    dve.tensor_tensor(m_a[:], sn_a[:], m_a[:], ALU.subtract).then_inc(s_dve, 1)
                    y, z = r3(1, 4, NB), r3(8, 4, NB)
                    link(dve.tensor_tensor(y, sx, par(3), ALU.mult))
                    link(dve.tensor_tensor(y, y, par(4), ALU.add))
                    for j in range(3):
                        link(dve.tensor_tensor(z, st[:, :, :, j], par(j), ALU.mult))
                        link(dve.tensor_tensor(y, y, z, ALU.add))
                    dve.nop().then_inc(s_conv, 1)
                if i == 2:
                    dve.wait_ge(s_pe, 1)
                    for g in range(2):
                        link(dve.tensor_tensor(r3(2 + g, 4, NB), ps[:, VB, 64 + 32 * g:96 + 32 * g].rearrange("p (f b) -> p f b", b=NB),
                                               par(5 + g), ALU.add))
                    dve.nop().then_inc(s_dve, 1)
                if i == 4:
                    dve.wait_ge(s_act, 5)
                    link(dve.tensor_scalar(w1[:, 2:4, :], w1[:, 2:4, :], 1.0, None, ALU.add))
                    link(dve.tensor_tensor(r3(2, 4, NB), r3(2, 4, NB), c4[:].unsqueeze(2).to_broadcast([P, 4, NB]), ALU.mult))
                    dve.nop().then_inc(s_dve, 1)
                    link(dve.scalar_tensor_tensor(out=w1[:, 3, :], in0=w1[:, 3, :], scalar=0.5, in1=w1[:, 1, :],
                                                  op0=ALU.mult, op1=ALU.mult))
                if i == 6:
                    dve.wait_ge(s_act, 6)
                    link(dve.tensor_tensor(w1[:, 9, :], w1[:, 4, :], w1[:, 4, :], ALU.mult))
                    dve.scalar_tensor_tensor(out=w1[:, 5, :], in0=w1[:, 9, :], scalar=1.0, in1=w1[:, 5, :],
                                             op0=ALU.add, op1=ALU.mult).then_inc(s_dve, 1)
                if i == 8:
                    dve.wait_ge(s_act, 7)
                    link(dve.tensor_tensor(w1[:, 3, :], w1[:, 3, :], w1[:, 5, :], ALU.mult))
                    link(dve.tensor_tensor(r3(4, 4, NB), r3(4, 4, NB), h0, ALU.mult))
                    link(dve.tensor_tensor(w1[:, 11, :], w1[:, 3, :], w1[:, 4, :], ALU.add))
                    link(dve.scalar_tensor_tensor(out=mix[:, 2:6, :], in0=r3(11, 4, NB), scalar=0.5,
                                                  in1=us[:, TI["gb0"]:TI["gb0"] + 4, :], op0=ALU.mult, op1=ALU.mult))
                if i == 9:
                    dve.wait_ge(s_act, 4)
                    num, dn, en = (w1[:, k, :].rearrange("p (j b c) -> p j b c", j=2, c=2) for k in (1, 2, 3))
                    for j in range(2):
                        for r in range(2):
                            hd, rw = 2 * j + r, slice(64 * r, 64 * r + 64)
                            dve.tensor_copy(num[rw, j], res_a[rw, :, 8 * j + 2 * hd:8 * j + 2 * hd + 2])
                            dve.tensor_copy(dn[rw, j], res_a[rw, :, 16 + 2 * hd:18 + 2 * hd])
                            link(dve.tensor_copy(en[rw, j], ds_a[rw, :, 2 * hd:2 * hd + 2]))
                    link(dve.tensor_tensor(w1[:, 2, :], w1[:, 2, :], w1[:, 3, :], ALU.add))
                    link(dve.tensor_tensor(en, en, us[:, TI["va0"]:TI["va0"] + 2, :].unsqueeze(3).to_broadcast([P, 2, NB, 2]),
                                           ALU.mult))
                    link(dve.tensor_tensor(w1[:, 1, :], w1[:, 1, :], w1[:, 3, :], ALU.add))
                    link(dve.reciprocal(w1[:, 2, :], w1[:, 2, :]))
                    link(dve.tensor_tensor(w1[:, 1, :], w1[:, 1, :], w1[:, 2, :], ALU.mult))
                    link(dve.scalar_tensor_tensor(out=oa, in0=num[:, :, :, 1], scalar=neglam[:, 0:1], in1=num[:, :, :, 0],
                                                  op0=ALU.mult, op1=ALU.add))
                    dve.tensor_tensor(w1[:, 8, 0:16], w1[:, 3, 0:16], w1[:, 3, 0:16], ALU.mult).then_inc(s_dve, 1)
                if i == 12:
                    dve.wait_ge(s_act, 8)
                    link(dve.reciprocal(w1[:, 9, 0:16], w1[:, 9, 0:16]))
                    link(dve.scalar_tensor_tensor(out=w1[:, 3, 0:16], in0=w1[:, 3, 0:16], scalar=gsub[:, 0:1], in1=w1[:, 9, 0:16],
                                                  op0=ALU.mult, op1=ALU.mult))
                    link(dve.scalar_tensor_tensor(out=mix[:, 0:2, :], in0=oa, scalar=0.5 * (1.0 - LAM_INIT),
                                                  in1=us[:, TI["ga0"]:TI["ga0"] + 2, :], op0=ALU.mult, op1=ALU.mult))
                if i == 13:
                    link(dve.tensor_scalar(w1[:, 0, :], w1[:, 0, :], 3.0, None, ALU.mult))
                    e_c = w1[:, 0, :].rearrange("p (b h) -> p b h", h=HC)
                    num, dn, en = (r3(j, 2, NB) for j in (1, 2, 4))
                    for j in range(2):
                        for r in range(2):
                            hd, rw = 2 * j + r, slice(64 * r, 64 * r + 64)
                            dve.tensor_copy(num[rw, j], res_c[rw, :, 4 * j + hd])
                            dve.tensor_copy(dn[rw, j], res_c[rw, :, 8 + hd])
                            link(dve.tensor_copy(en[rw, j], e_c[rw, :, hd]))
                    link(dve.tensor_tensor(dn, dn, en, ALU.add))
                    link(dve.tensor_tensor(en, en, us[:, TI["vc0"]:TI["vc0"] + 2, :], ALU.mult))
                    link(dve.tensor_tensor(num, num, en, ALU.add))
                    link(dve.reciprocal(dn, dn))
                    link(dve.tensor_tensor(num, num, dn, ALU.mult))
                    dve.scalar_tensor_tensor(out=mix[:, 6:8, :], in0=num, scalar=0.5, in1=us[:, TI["gc0"]:TI["gc0"] + 2, :],
                                             op0=ALU.mult, op1=ALU.mult).then_inc(smix, 1)
                if i == 15:
                    dve.wait_ge(sxh_done, 1)
                    dve.wait_ge(smix, 1)
                    dve.tensor_tensor(sxl[:], mix, sxh[:].bitcast(F32), ALU.subtract).then_inc(sxl_done, 1)

            for u in range(NU + 1):
                if u < NU:
                    mask_scores(u)
                if u >= 1:
                    probs(u - 1)
                if u < NU:
                    sample_events(PSTEPS + 2 * u)
                    sample_events(PSTEPS + 2 * u + 1)
                sample_last(u - SAMPLE_AT)
                for part in range(2):
                    if u - part in LRU_AT:
                        conv(LRU_AT[u - part], part)
                if u - 6 in LRU_AT:
                    f = LRU_AT[u - 6]
                    dve.wait_ge(item_read, OTHER_NO["gate", f, 3] + 1)
                    dve.scalar_tensor_tensor(out=TMP[2][:, 0:S], in0=TMP[2][:, 0:S], scalar=1.0, in1=TMP[0][:, 0:S],
                                             op0=ALU.add, op1=ALU.mult).then_inc(lru_xi, 1)
                if u - 7 in LRU_AT:
                    f = LRU_AT[u - 7]
                    dve.wait_ge(lru_a, 2 * f + 2)
                    dve.wait_ge(lru_sq, f + 1)
                    dve.scalar_tensor_tensor(out=TMP[1][:, 0:S], in0=tile_of[f"xb{f}"][:, 0:S], scalar=1.0,
                                             in1=TMP[1][:, 0:S], op0=ALU.add, op1=ALU.mult).then_inc(lru_om, 1)
                if u - 10 in LRU_AT:
                    f = LRU_AT[u - 10]
                    h = tile_of[f"xb{f}"]
                    dve.wait_ge(lru_in, f + 1)
                    dve.tensor_tensor_scan(h[:, 0:S], TMP[3][:, 0:S], TMP[2][:, 0:S], 0.0, ALU.mult, ALU.add)\
                       .then_inc(lru_h, 1)
                    dve.wait_ge(lru_h, f + 1)
                    dve.tensor_scalar(w1[:, 10, f:f + 1], h[:, S - 1:S], 0.5, None, ALU.mult).then_inc(lru_last, 1)
                for i in range(4):
                    if u - 4 - i in NORM_AT:
                        p = NORM_AT[u - 4 - i]
                        part = TMP[1][:, i * 256:(i + 1) * 256]
                        dve.wait_ge(item_read, OTHER_NO["norm", p, 0] + 1)
                        link(dve.reciprocal(part, part))
                if u - 7 in NORM_AT:
                    p = NORM_AT[u - 7]
                    link(dve.scalar_tensor_tensor(out=TMP[1][:, 0:S], in0=TMP[1][:, 0:S], scalar=gsub[:, 0:1],
                                                  in1=tile_of[f"qa{p}"][:, 0:S], op0=ALU.mult, op1=ALU.mult))
                if u - 8 in NORM_AT:
                    p = NORM_AT[u - 8]
                    dve.wait_ge(norm_gate_in, 16 * (p + 1))
                    dve.scalar_tensor_tensor(out=tile_of[f"qa{p}"][:, 0:S], in0=TMP[1][:, 0:S],
                                             scalar=0.5 * (1.0 - LAM_INIT), in1=TMP[2][:, 0:S],
                                             op0=ALU.mult, op1=ALU.mult).then_inc(nrm_done, 1)

            for k, n in enumerate(MIX):
                if k == 0:
                    dve.wait_ge(attended, NU)
                if k == EARLY_MIX:
                    t = tile_of["qc1"]
                    dve.wait_ge(core_out, NU)
                    dve.wait_ge(c_gate_in[1], 16)
                    dve.tensor_tensor(t[:, 0:S], t[:, 0:S], TMP[0][:, 0:S], ALU.mult).then_inc(mix_c, 1)
                dve.wait_ge(mh_done, k + 1)
                if k == 6:
                    dve.wait_ge(mix_c, 2)
                dve.scalar_tensor_tensor(out=ml[:, k, NB:SW], in0=tile_of[n][:, 0:S], scalar=mix_scale(n),
                                         in1=mh[:, k, NB:SW].bitcast(F32), op0=ALU.mult, op1=ALU.subtract)\
                   .then_inc(ml_done, 1)
            dve.wait_ge(gpost_in, 16)
            for s in range(NQ + 1):
                n = P if s else NB
                y = y_sb[s % 2][0:n, :]
                dve.wait_ge(y_rt, s + 1)
                link(dve.reciprocal(yrs[0:n, s:s + 1], yrs[0:n, s:s + 1]))
                dve.scalar_tensor_tensor(out=y, in0=y_before(s), scalar=yrs[0:n, s:s + 1], in1=g_post[0:n, :],
                                         op0=ALU.mult, op1=ALU.mult).then_inc(y_nrm, 1)
                dve.wait_ge(y_nrm, s + 1)
                dve.wait_ge(res_in[s % 2], 16 * (s // 2 + 1))
                dve.tensor_tensor(y, y, x_res[s % 2][0:n, :], ALU.add).then_inc(y_add, 1)

        @block.tensor
        def _(pe):
            pe.wait_ge(first_in, 32)

            def early_q(t):
                pe.wait_ge(wl_done, t + 1)
                pe.wait_ge(xl_done, 2)
                out = ps[:, JB, NB * t:NB * (t + 1)]
                for kt in range(KT):
                    pe.matmul(out, wh[t][:, kt, :], xh[:, kt, S:SW], start=(kt == 0), stop=False)
                    pe.matmul(out, wh[t][:, kt, :], xl[:, kt, S:SW], start=False, stop=False)
                    ins = pe.matmul(out, wl[t][:, kt, :], xh[:, kt, S:SW], start=False, stop=(kt == KT - 1))
                ins.then_inc(early, 1)

            for i, s in enumerate(X_ORDER):
                n = P if s < NQ else NB
                pe.wait_ge(xn_done, i + 1)
                for h in range(2):
                    u = 2 * i + h
                    if u >= 5:
                        pe.wait_ge(xl_done, u - 4)
                    for k in range(4):
                        f = (4 * h + k) * P
                        ins = pe.transpose(ps[:, u % 5, k * n:(k + 1) * n], xn[i % 2][0:n, f:f + P], ident[0:n, 0:n])
                    ins.then_inc(x_turned, 1)
                if i in (2, 4):
                    early_q(i // 2 - 1)
                if i == 6:
                    pe.wait_ge(early_out, 1)
                    for t in range(2):
                        ins = pe.transpose(ps[0:NB, JB, t * P:(t + 1) * P], us[:, t, :], ident[:])
                    ins.then_inc(early, 1)
            pe.wait_ge(early_out, 2)

            def job_pe(ji):
                _, k, arg, h = JOBS[ji]
                if ji >= 1:
                    pe.wait_ge(job_out, ji)
                if k == "param":
                    pe.wait_ge(consts_in, 16 * NCONST)
                    for f in range(4):
                        ins = pe.transpose(ps[:, JB, 8 * f:8 * f + 8], prow[:, f * P:(f + 1) * P], ident[0:8, 0:8])
                elif k == "state":
                    for f in range(4):
                        ins = pe.transpose(ps[:, JB, 32 * f:32 * f + 32], srow[:, f * P:(f + 1) * P], ident[0:32, 0:32])
                elif k == "rows":
                    pe.wait_ge(evac, 3 * (4 * arg + 4))
                    for i in range(4):
                        ins = pe.transpose(ps[0:NB, JB, i * P:(i + 1) * P], us[:, 4 * arg + i, :], ident[:])
                elif k == "tail":
                    for f in range(4):
                        ins = pe.transpose(ps[0:3, JB, f * P:(f + 1) * P], tile_of[f"xb{f}"][:, S - 3:S], ident[:])
                elif k == "turn":
                    t = TI[arg]
                    pe.wait_ge(evac, 3 * (t + 1))
                    for i in range(4):
                        c = (4 * h + i) * P
                        ins = pe.transpose(ps[:, JB, i * P:(i + 1) * P], dest(t)[:, c:c + P], ident[:])
                elif k == "cpv":
                    b = arg
                    pe.wait_ge(exc_done, b + 1)
                    pe.wait_ge(vc_in[b % 2], 48 * (b // 2 + 1))
                    for i in range(3):
                        ins = pe.matmul(ps[32 * i:32 * i + HC, JB, 0:W_BR], ex_c[b % 2][:, i, :], vc[b % 2][:, i, :],
                                        start=True, stop=True)
                ins.then_inc(job, 1)

            in_rb = [0, 0, 0]

            def results_free():
                for s_, n_ in zip((core_out, res_done, res_c_done), in_rb):
                    if n_:
                        pe.wait_ge(s_, n_)

            def pick_c(b):
                pe.wait_ge(job_out, JOB_NO["cpv", b, 0] + 1)
                results_free()
                in_rb[2] += 1
                pe.wait_ge(dsc_done, b + 1)
                for j in range(2):
                    pe.matmul(ps[:, RB, 32 + 4 * j:36 + 4 * j], acc_c[:, j * P:(j + 1) * P], sel[:, 8:12], start=True, stop=True)
                pe.matmul(ps[:, RB, 40:44], ones[:], ds_c[:, b, :], start=True, stop=True).then_inc(picked_c, 1)

            def pick(b):
                pe.wait_ge(acc_out, b + 1)
                results_free()
                in_rb[1] += 1
                pe.wait_ge(ds_done, b + 1)
                for j in range(2):
                    pe.matmul(ps[:, RB, 8 * j:8 * j + 8], acc[:, j * P:(j + 1) * P], sel[:, 0:8], start=True, stop=True)
                pe.matmul(ps[:, RB, 16:24], ones[:], ds_a[:, b, :], start=True, stop=True).then_inc(picked, 1)

            def sample_events(step):
                m = V_AT.get(step)
                if m is not None:
                    b, c = divmod(m, NCH)
                    pe.wait_ge(v_in[m % 3], 16 * (m // 3 + 1))
                    if c == 0:
                        pe.wait_ge(ex_done, b + 1)
                        if b >= 1:
                            pe.wait_ge(acc_out, b)
                    for i in range(CH):
                        o_ = ps[32 * i:32 * i + HCA, VB, 0:W_BR]
                        ins = pe.matmul(o_, ex[b % 2][:, CH * c + i, :], vbuf[m % 3][:, i, :],
                                        start=(c == 0), stop=(c == NCH - 1))
                    ins.then_inc(v_used, 1)
                if step in PICK_AT:
                    pick(PICK_AT[step])
                b = C_STEP.get(step - 8)
                if b is not None:
                    pick_c(b)

            for step in range(PSTEPS):
                t, kt = divmod(step, KT)
                if kt == 0:
                    pe.wait_ge(wl_done, t + 1)
                    if t == 0:
                        pe.wait_ge(xl_done, 18)
                for c in range(3):
                    if kt == 0 and 3 * t + c >= 5:
                        bt, bc = divmod(3 * t + c - 5, 3)
                        if kind(bt) == "gate":
                            pe.wait_ge(gated, gate_no(bt, bc))
                        else:
                            pe.wait_ge(evac, 3 * bt + bc + 1)
                    pr = ps[:, bank_of(t, c), 0:CW]
                    cols = slice(c * CW, (c + 1) * CW)
                    pe.matmul(pr, wh[t % 2][:, kt, :], xh[:, kt, cols], start=(kt == 0), stop=False)
                    pe.matmul(pr, wh[t % 2][:, kt, :], xl[:, kt, cols], start=False, stop=False)
                    ins = pe.matmul(pr, wl[t % 2][:, kt, :], xh[:, kt, cols], start=False, stop=(kt == KT - 1))
                    if kt == KT - 1:
                        ins.then_inc(proj, 1)
                sample_events(step)
                ji = JOB_AT.get(step)
                if ji is not None:
                    job_pe(ji)

            stage1_over(pe)

            def scores(u):
                h, q = UNITS[u]
                w = (q + 1) * P
                sl = stack[h % 2]
                if u == 0:
                    pe.wait_ge(first_stack, 16 * 4)
                if u == FIRST // P or (q == 0 and h >= 1):
                    pe.wait_ge(stack_in[h % 2], stacked(h))
                for c in range(2 if h < HA else 1):
                    it = ("s", u, c)
                    keep_free(pe, it)
                    out = score_bank(it)
                    for k0 in range(0, w, 512):
                        k1 = min(w, k0 + 512)
                        if h < HA:
                            ins = pe.matmul(out[:, k0:k1], sl[2 * c][:, q * P:(q + 1) * P], sl[2 * c + 1][:, k0:k1],
                                            start=True, stop=True)
                        else:
                            pe.matmul(out[:, k0:k1], sl[0][:, q * P:(q + 1) * P], sl[1][:, k0:k1], start=True, stop=False)
                            ins = pe.matmul(out[:, k0:k1], sl[0][:, q * P:(q + 1) * P], sl[2][:, k0:k1],
                                            start=False, stop=True)
                    ins.then_inc(scored, 1)

            def turn(u):
                h, q = UNITS[u]
                pe.wait_ge(pd_done, u + 1)
                for g in range(2 if q >= 4 else 1):
                    i = GROUP_NO[u, g]
                    if i >= 2:
                        pe.wait_ge(pt_out, i - 1)
                    for k in range(min(4, q + 1 - 4 * g)):
                        c = (4 * g + k) * P
                        ins = pe.transpose(ps[:, 4 + i % 2, k * P:(k + 1) * P], E[2 * u % 4][:, c:c + P], ident[:])
                    ins.then_inc(turned, 1)

            def attend(u):
                h, q = UNITS[u]
                r = 64 * (h % 2)
                pe.wait_ge(pt_out, GROUP_NO[u, 1 if q >= 4 else 0] + 1)
                results_free()
                in_rb[0] += 1
                if u == 0:
                    pe.wait_ge(va_in, 16)
                if h == HA and q == 0:
                    pe.wait_ge(vc_nat_in, 16)
                v = v_a if h < HA else v_c
                f = (h % 4) * 64
                for k in range(q + 1):
                    ins = pe.matmul(ps[r:r + 64, RB, 128:256], v[:, k, f:f + 64],
                                    PT[u % 2][:, k, :], start=(k == 0), stop=(k == q))
                ins.then_inc(attended, 1)

            for u in range(-1, NU + 2):
                if u + 1 < NU:
                    scores(u + 1)
                if u >= 2:
                    attend(u - 2)
                if 1 <= u <= NU:
                    turn(u - 1)
                for i in range(4):
                    if u - 2 - i in LRU_AT:
                        f, w, k0 = LRU_AT[u - 2 - i], i // 2, (i % 2) * 512
                        it = ("gate", f, i)
                        pe.wait_ge(conv_done, f + 1)
                        keep_free(pe, it)
                        pe.matmul(score_bank(it)[:, 0:512], bdiag[:, f, w, :], TMP[0][:, k0:k0 + 512],
                                  start=True, stop=True).then_inc(scored, 1)
                if u - 2 in NORM_AT:
                    it = ("norm", NORM_AT[u - 2], 0)
                    pe.wait_ge(sq_done, NORM_AT[u - 2] + 1)
                    keep_free(pe, it)
                    for k0 in (0, 512):
                        ins = pe.matmul(score_bank(it)[:, k0:k0 + 512], bones[:], TMP[0][:, k0:k0 + 512],
                                        start=True, stop=True)
                    ins.then_inc(scored, 1)
                if u - SAMPLE_AT == 1:
                    pe.wait_ge(acc_out, NB)
                    pe.wait_ge(s_conv, 1)
                    for g in range(2):
                        for f in range(4):
                            ins = pe.matmul(ps[:, VB, 64 + 32 * g + 8 * f:72 + 32 * g + 8 * f], bdiag[:, f, g, :],
                                            w1[:, 1, 8 * f:8 * f + 8], start=True, stop=True)
                    ins.then_inc(s_pe, 1)
                if u - SAMPLE_AT == 10:
                    pe.wait_ge(s_dve, 9)
                    pe.matmul(ps[:, VB, 64:80], bones[:], w1[:, 8, 0:16], start=True, stop=True).then_inc(s_pe, 1)
                if u in YS_AT:
                    n, i = divmod(YS_AT[u], 4)
                    if n == 0 and i == 0:
                        pe.wait_ge(s_act, 8)
                        pe.wait_ge(sxl_done, 1)
                    if n == 1 and i == 0:
                        pe.wait_ge(ys_out, 1)
                    out, w_ = ps[0:NB, VB, :], slice(n * 512, (n + 1) * 512)
                    for k in (2 * i, 2 * i + 1):
                        pe.wait_ge(wol_done, k + 1)
                        pe.matmul(out, sxh[:, k, :], wo[k][:, 0, w_], start=(k == 0), stop=False)
                        pe.matmul(out, sxh[:, k, :], wo[k][:, 1, w_], start=False, stop=False)
                        ins = pe.matmul(out, sxl[:, k, :], wo[k][:, 0, w_], start=False, stop=(k == KT - 1))
                    if i == 3:
                        ins.then_inc(ys_part, 1)
                if 0 <= u < NU:
                    sample_events(PSTEPS + 2 * u)
                    sample_events(PSTEPS + 2 * u + 1)

            pe.wait_ge(core_out, NU)
            for s in range(NQ):
                cols = slice(NB + s * P, NB + (s + 1) * P)
                if s >= 3:
                    pe.wait_ge(y_nrm, s - 1)
                for k in range(KT):
                    if s == 0:
                        pe.wait_ge(ml_done, k + 1)
                        pe.wait_ge(wol_done, k + 1)
                    for n in range(2):
                        out = flat[:, (s % 3) * D + n * 512:(s % 3) * D + (n + 1) * 512]
                        w_ = slice(n * 512, (n + 1) * 512)
                        pe.matmul(out, mh[:, k, cols], wo[k][:, 0, w_], start=(k == 0), stop=False)
                        pe.matmul(out, mh[:, k, cols], wo[k][:, 1, w_], start=False, stop=False)
                        ins = pe.matmul(out, ml[:, k, cols], wo[k][:, 0, w_], start=False, stop=(k == KT - 1))
                ins.then_inc(y_done, 1)


_INS = ["x_prompt", "x_sample", "cache_a_k", "cache_a_v", "state_conv", "state_lru", "cache_c_k", "cache_c_v",
        "page_table", "ln_pre", "ln_post", "w_in", "w_out", "lam_q1", "lam_k1", "lam_q2", "lam_k2", "subln_g",
        "conv_w", "conv_b", "w_rgate", "b_rgate", "w_igate", "b_igate", "lru_lambda"]
_OUTS = [(1, S, D), (NB, 1, D), (1, 1, S, HA, 64), (1, 1, S, HA, 64), (1, NB, 1, HA, 64), (1, NB, 1, HA, 64),
         (1, 1, 3, DL), (1, NB, 3, DL), (1, 1, DL), (1, NB, DL), (1, 1, S, HC, DHC), (1, 1, S, HC, DHC),
         (1, NB, 1, HC, DHC), (1, NB, 1, HC, DHC)]


def _constants():
    import numpy as np

    i, j = np.arange(P)[:, None], np.arange(P)[None, :]
    mask_a = np.zeros((P, S), np.float32)
    mask_a[:, S - P:] = np.where(j <= i, 0.0, NEG)
    mask_c = np.zeros((P, S), np.float32)
    for b in range(NQ):
        dist = P * (NQ - 1 - b) + i - j
        count = sum(((dist >= 0) & (dist <= win) & (dist % dil == 0)).astype(int)
                    for win, dil in ((128, 1), (512, 4), (2048, 16)))
        mask_c[:, b * P:(b + 1) * P] = np.where(count > 0, np.log(np.maximum(count, 1)) / SCALE_C, NEG)
    sel = np.zeros((P, 16), np.float32)
    for q in range(4):
        for h in range(HCA):
            sel[32 * q + h, h] = 1.0
        for h in range(HC):
            if q < 3:
                sel[32 * q + h, 8 + h] = 1.0
    return {"c_ident": np.eye(P, dtype=np.float32), "c_bones": np.where(i // 64 == j // 64, 1.0 / 64, 0.0).astype(np.float32),
            "c_sel": sel, "c_mask_a": mask_a, "c_mask_c": mask_c.astype(np.float32),
            "c_quarter": (np.arange(P) % QPP).astype(np.float32).reshape(P, 1)}


def kernel(**inputs):
    import numpy as np
    import concourse.bacc as bacc
    from concourse.bass_utils import run_bass_kernel_spmd

    nc = bacc.Bacc("TRN2", target_bir_lowering=False, num_devices=1, dynamic_dma_scratch_size=4096)
    arrays, aps = {}, {}
    given = {n: np.ascontiguousarray(inputs[n]) for n in _INS}
    for name, arr in {**given, **_constants()}.items():
        arrays[f"in_{name}"] = arr
        aps[name] = nc.dram_tensor(f"in_{name}", arr.shape, mybir.dt.from_np(arr.dtype), kind="ExternalInput").ap()
    outs = [nc.dram_tensor(f"out_{i}", list(s), F32, kind="ExternalOutput").ap() for i, s in enumerate(_OUTS)]
    build(nc, aps, outs)
    r = run_bass_kernel_spmd(nc, [arrays], core_ids=[0])
    return tuple(r.results[0][f"out_{i}"] for i in range(len(_OUTS)))
```
